# Optimizing a Trainium2 kernel written in Bass

```python
import jax, jax.numpy as jnp
from jax import lax
import numpy as np

D_MODEL = 2048
BATCH = 1
SEQ = 512
DEPTH = 1

CHUNK = 64
D_MIX = D_MODEL
SB_HEADS = 8
SB_HEAD_DIM = 128
SB_WIDTH = SB_HEADS * SB_HEAD_DIM
SB_BLOCK = 128
SG_GROUPS = 8
SG_WIDTH = D_MIX - SB_WIDTH
SG_GROUP_DIM = SG_WIDTH // SG_GROUPS
SG_BLOCK = 128
IN_WIDTH = 3 * SB_WIDTH + 2 * SG_WIDTH
PEER_HEADS = 8
PEER_N_KEYS = 128
PEER_N_EXPERTS = PEER_N_KEYS * PEER_N_KEYS
PEER_KEY_DIM = 128
PEER_TOPK = 16
PEER_TOKEN_BLOCK = 128
RMS_EPS = 1e-6

kernel_name = 'hybrid_stickbreak_gmlp_peer'

def rms_norm(x, gain=None):
    xf = x.astype(jnp.float32)
    y = xf * lax.rsqrt(jnp.mean(xf * xf, axis=-1, keepdims=True) + RMS_EPS)
    if gain is not None:
        y = y * gain.astype(jnp.float32)
    return y.astype(x.dtype)

def stick_breaking_attention(q, k, v):
    b, s, h, d = q.shape
    scale = d ** -0.5
    outs = []
    for i in range(s // SB_BLOCK):
        start, end = i * SB_BLOCK, (i + 1) * SB_BLOCK
        z = jnp.einsum('bqhd,bkhd->bhqk', q[:, start:end], k[:, :end]).astype(jnp.float32) * scale
        t_pos = start + jnp.arange(SB_BLOCK)[:, None]
        s_pos = jnp.arange(end)[None, :]
        strict = s_pos < t_pos
        log_rem = jnp.where(strict, jax.nn.log_sigmoid(-z), 0.0)
        tail = lax.cumsum(log_rem, axis=3, reverse=True) - log_rem
        w = jnp.where(strict, jnp.exp(jax.nn.log_sigmoid(z) + tail), 0.0)
        outs.append(jnp.einsum('bhqk,bkhd->bqhd', w.astype(v.dtype), v[:, :end]))
    return jnp.concatenate(outs, axis=1)

def chunked_spatial_gating(u, v, w_s, b_s, g_v):
    b, s, g, c = u.shape
    n = s // SG_BLOCK
    chunk_id = jnp.arange(SG_BLOCK) // CHUNK
    mask = chunk_id[:, None] >= chunk_id[None, :]
    w = jnp.where(mask[None], w_s, 0.0).astype(v.dtype)
    vb = rms_norm(v, g_v).reshape(b, n, SG_BLOCK, g, c)
    mixed = jnp.einsum('gpq,bnqgc->bnpgc', w, vb) + b_s.T[None, None, :, :, None].astype(v.dtype)
    return u * mixed.reshape(b, s, g, c)

def peer_ffn(h, w_query, sub_keys, expert_u, expert_v):
    b, s, d = h.shape
    t = b * s
    hf = h.reshape(t, d)
    q = rms_norm((hf @ w_query).reshape(t, PEER_HEADS, 2 * PEER_KEY_DIM))
    q = q.reshape(t, PEER_HEADS, 2, PEER_KEY_DIM)
    s1 = jnp.einsum('thk,nk->thn', q[:, :, 0], sub_keys[0]).astype(jnp.float32)
    s2 = jnp.einsum('thk,nk->thn', q[:, :, 1], sub_keys[1]).astype(jnp.float32)
    v1, i1 = lax.top_k(s1, PEER_TOPK)
    v2, i2 = lax.top_k(s2, PEER_TOPK)
    n_cand = PEER_TOPK * PEER_TOPK
    cand_score = (v1[..., :, None] + v2[..., None, :]).reshape(t, PEER_HEADS, n_cand)
    cand_idx = (i1[..., :, None] * PEER_N_KEYS + i2[..., None, :]).reshape(t, PEER_HEADS, n_cand)
    top_score, top_pos = lax.top_k(cand_score, PEER_TOPK)
    expert_idx = jnp.take_along_axis(cand_idx, top_pos, axis=-1)
    gate = jax.nn.softmax(top_score, axis=-1)
    nb = t // PEER_TOKEN_BLOCK
    k_tot = PEER_HEADS * PEER_TOPK

    def block(args):
        hb, idx, gb = args
        u_sel = jnp.take(expert_u, idx, axis=0)
        act = jax.nn.gelu(jnp.einsum('tkd,td->tk', u_sel, hb).astype(jnp.float32), approximate=False) * gb
        v_sel = jnp.take(expert_v, idx, axis=0)
        return jnp.einsum('tk,tkd->td', act.astype(hb.dtype), v_sel)

    out = lax.map(block, (hf.reshape(nb, PEER_TOKEN_BLOCK, d),
                          expert_idx.reshape(nb, PEER_TOKEN_BLOCK, k_tot),
                          gate.reshape(nb, PEER_TOKEN_BLOCK, k_tot)))
    return out.reshape(b, s, d)

def setup_inputs(seed: int = 0) -> dict:
    key = jax.random.key(seed)
    ks = jax.random.split(key, 16)
    f32 = jnp.float32
    nrm = lambda k, shape, scale: jax.random.normal(k, shape, f32) * scale
    gain = lambda k, shape: 1.0 + 0.02 * jax.random.normal(k, shape, f32)
    return {
        'x': jax.random.normal(ks[0], (BATCH, SEQ, D_MODEL), f32),
        'norm_mix': gain(ks[1], (DEPTH, D_MODEL)),
        'w_in': nrm(ks[2], (DEPTH, D_MODEL, IN_WIDTH), D_MODEL ** -0.5),
        'q_norm': gain(ks[3], (DEPTH, SB_HEAD_DIM)),
        'k_norm': gain(ks[4], (DEPTH, SB_HEAD_DIM)),
        'sg_norm': gain(ks[5], (DEPTH, SG_GROUPS, SG_GROUP_DIM)),
        'sg_w': nrm(ks[6], (DEPTH, SG_GROUPS, SG_BLOCK, SG_BLOCK), SG_BLOCK ** -0.5),
        'sg_b': 1.0 + 0.1 * jax.random.normal(ks[7], (DEPTH, SG_GROUPS, SG_BLOCK), f32),
        'out_norm_sb': gain(ks[8], (DEPTH, SB_WIDTH)),
        'out_norm_sg': gain(ks[9], (DEPTH, SG_WIDTH)),
        'w_out': nrm(ks[10], (DEPTH, D_MIX, D_MODEL), D_MIX ** -0.5),
        'norm_ffn': gain(ks[11], (DEPTH, D_MODEL)),
        'peer_w_query': nrm(ks[12], (DEPTH, D_MODEL, PEER_HEADS * 2 * PEER_KEY_DIM), D_MODEL ** -0.5),
        'peer_sub_keys': nrm(ks[13], (DEPTH, 2, PEER_N_KEYS, PEER_KEY_DIM), PEER_KEY_DIM ** -0.5),
        'peer_u': nrm(ks[14], (DEPTH, PEER_N_EXPERTS, D_MODEL), D_MODEL ** -0.5),
        'peer_v': nrm(ks[15], (DEPTH, PEER_N_EXPERTS, D_MODEL), PEER_HEADS ** -0.5),
    }

def reference(x, norm_mix, w_in, q_norm, k_norm, sg_norm, sg_w, sg_b, out_norm_sb, out_norm_sg,
              w_out, norm_ffn, peer_w_query, peer_sub_keys, peer_u, peer_v):
    b, s, _ = x.shape
    for layer in range(DEPTH):
        h = rms_norm(x, norm_mix[layer])
        proj = h @ w_in[layer]
        q, k, v, u_g, v_g = jnp.split(
            proj, [SB_WIDTH, 2 * SB_WIDTH, 3 * SB_WIDTH, 3 * SB_WIDTH + SG_WIDTH], axis=-1)
        q = rms_norm(q.reshape(b, s, SB_HEADS, SB_HEAD_DIM), q_norm[layer])
        k = rms_norm(k.reshape(b, s, SB_HEADS, SB_HEAD_DIM), k_norm[layer])
        v = v.reshape(b, s, SB_HEADS, SB_HEAD_DIM)
        y_sb = stick_breaking_attention(q, k, v).reshape(b, s, SB_WIDTH)
        u_g = jax.nn.gelu(u_g, approximate=False).reshape(b, s, SG_GROUPS, SG_GROUP_DIM)
        v_g = jax.nn.gelu(v_g, approximate=False).reshape(b, s, SG_GROUPS, SG_GROUP_DIM)
        y_sg = chunked_spatial_gating(u_g, v_g, sg_w[layer], sg_b[layer], sg_norm[layer]).reshape(b, s, SG_WIDTH)
        y = jnp.concatenate([rms_norm(y_sb, out_norm_sb[layer]), rms_norm(y_sg, out_norm_sg[layer])], axis=-1)
        x = x + y @ w_out[layer]
        h2 = rms_norm(x, norm_ffn[layer])
        x = x + peer_ffn(h2, peer_w_query[layer], peer_sub_keys[layer], peer_u[layer], peer_v[layer])
    return x


_drawn_inputs = setup_inputs


def setup_inputs(seed=0):
    import zlib

    import numpy as np

    out = dict(_drawn_inputs(seed))
    spreads = {}
    factors = {'q_norm': 5.451,
     'k_norm': 5.368,
     'sg_norm': 4.2,
     'out_norm_sb': 3.449,
     'out_norm_sg': 3.451,
     'norm_ffn': 3.034}
    for name, (base, spread) in spreads.items():
        noise = np.random.default_rng([zlib.crc32(name.encode()), seed]).standard_normal(out[name].shape)
        drawn = base * np.exp(spread * noise) if base else spread * noise
        out[name] = __import__('jax').numpy.asarray(drawn.astype(out[name].dtype))
    for name, factor in factors.items():
        out[name] = (out[name] * factor).astype(out[name].dtype)
    return out
```

```python
from contextlib import ExitStack

import concourse.bass as bass
from concourse import mybir

ALU = mybir.AluOpType
ACT = mybir.ActivationFunctionType
AX_X = mybir.AxisListType.X
F32 = mybir.dt.float32
F32R = mybir.dt.float32r
U32 = mybir.dt.uint32

P = 128
SEQ = 512
TT = SEQ // P
D = 2048
KD = D // P
HEADS = 8
HD = 128
WIDTH = HEADS * HD
PARTS = 5
Q_PART, K_PART, V_PART, U_PART, G_PART = range(PARTS)
NBANK = 8
BANK = 512
EPS = 1e-6
BIG = 1.0e30

PH = 8
NK = 128
TOPK = 16
NEG = -3.0e38

PIECE = 2048
KQ = 4
IN_CHUNKS = PARTS * WIDTH // BANK
IN_PIECES = IN_CHUNKS * KQ
MM_PIECES = D // BANK * KQ
P_OUT = IN_PIECES
P_QUERY = P_OUT + MM_PIECES
P_PEER = P_QUERY + MM_PIECES
GROUP = 4
N_GROUPS = NK // GROUP
RING_SLOTS = 2
SCALE = float(HD) ** -0.5

IN_NORM, MIX_NORM, FFN_NORM = range(3)


def layer(nc, x, nm, nf, ny, qn, kn, sgn, sgw, sgb, keys, w_in, w_out, w_q, pu, pv, out):
    gates = nc.dram_tensor("gates_scratch", (NK, NK, SEQ), F32).ap()

    base = [16512]

    def at(name, shape, dt, kb):
        return nc.alloc_sbuf_tensor_at(name, shape, dt, offset=base[0] + int(kb * 1024))

    actT_hi = at("actT_hi", [P, KD, SEQ], F32R, 0)
    actT_lo = at("actT_lo", [P, KD, SEQ], F32R, 32)
    raw = at("ring_raw", [P, RING_SLOTS, PIECE], F32, 64)
    hi = at("ring_hi", [P, RING_SLOTS, PIECE], F32R, 80)
    lo = at("ring_lo", [P, RING_SLOTS, PIECE], F32R, 96)
    proj = at("proj", [P, PARTS, TT, WIDTH], F32, 112)
    x0 = at("x0", [P, TT, D], F32, 112)
    junk0 = at("junk0", [P, D], F32, 160)
    qk_n = at("qk_n", [P, 2, 2, TT, HD], F32, 0)
    qkT = at("qkT", [P, 2, 2, SEQ], F32, 8)
    v_h = at("v_h", [P, 2, TT, HD], F32, 16)
    sp_t = at("sp_t", [P, 2, 1280], F32, 20)
    sp = at("sp", [P, 2, 1280], F32, 30)
    w_att = at("w_att", [P, 2, 1280], F32, 40)
    x1 = at("x1", [P, TT, D], F32, 128)
    x1n = at("x1n", [P, TT, D], F32, 160)
    junk1 = at("junk1", [P, D], F32, 176)
    junk2 = at("junk2", [P, D], F32, 112)
    sqh = at("sqh", [P, PH, SEQ], F32, 112)
    qT = at("qT", [P, 2 * PH, SEQ], F32, 160)
    s_sb = at("s_sb", [P, 2 * PH, NK], F32, 64)
    cand = at("cand", [P, PH, TOPK, TOPK], F32, 72)
    eq = at("eq", [P, PH * TOPK, TOPK], F32, 80)
    v12 = at("v12", [P, 2 * PH, TOPK], F32, 88)
    i12u = at("i12u", [P, 2 * PH, TOPK], U32, 89)
    i12f = at("i12f", [P, 2 * PH, TOPK], F32, 90)
    tv = at("tv", [P, PH, TOPK], F32, 91)
    tpos = at("tpos", [P, PH, TOPK], U32, 91.5)
    posu = at("posu", [P, 2, PH * TOPK], U32, 92)
    posf = at("posf", [P, 2, PH * TOPK], F32, 93)
    gate_e = at("gate_e", [P, PH, TOPK], F32, 94)
    gate_s = at("gate_s", [P, 2, PH], F32, 94.5)
    sel = at("sel", [P, 3, P], F32, 95)
    gbuf = at("gbuf", [P, NK, P], F32, 64)
    hot_a = at("hot_a", [P, 16, NK], F32, 160)
    hot_b = at("hot_b", [P, 16, NK], F32, 168)
    gch = at("gate_chunk", [P, GROUP, SEQ], F32, 112)
    gelu = at("gelu", [P, 2, SEQ], F32, 120)
    act_f = at("act_f", [P, 2, SEQ], F32, 124)
    a_hi = at("a_hi", [P, 2, GROUP, SEQ], F32R, 160)
    a_lo = at("a_lo", [P, 2, GROUP, SEQ], F32R, 176)
    ident = at("ident", [P, P], F32, 192)
    tri = at("tri", [P, P], F32, 192.5)
    neg1 = at("neg1", [P, P], F32, 193)
    keep = at("keep", [P, P], F32, 193.5)
    block_m = at("block_m", [P, P], F32, 194)
    iota = at("iota128", [P, NK], F32, 194.5)
    keysT = at("keysT", [P, 2, NK], F32, 195)
    sq = at("sq", [P, 2, BANK], F32, 196)
    selT = at("selT", [P, 3, SEQ], F32, 200)
    iota16 = at("iota16", [P, TOPK], F32, 206)
    small = at("small", [P, 110], F32, 206.0625)
    stats = at("stats", [P, PARTS, TT, HEADS], F32, 206.5)
    gains = small[:, 0:48].rearrange("p (s k) -> p s k", s=3)
    qgain, kgain, sgb_s = small[:, 48:49], small[:, 49:50], small[:, 50:58]
    ss = small[:, 58:66]
    rq = small[:, 66:98].rearrange("p (t h) -> p t h", t=TT)
    tick = small[:, 98:99]
    sgw_s = at("sgw_s", [P, HEADS, P], F32, 52)
    sgn_s = at("sgn_s", [P, WIDTH], F32, 56)

    with ExitStack() as ctx:
        ps = ctx.enter_context(nc.psum_tensor("ps", [P, NBANK, BANK], F32))

        def sem(name):
            return ctx.enter_context(nc.semaphore(name))

        s_par = sem("params_loaded")
        s_x = [sem(f"x_loaded_{t}") for t in range(TT)]
        s_const = sem("constants_made")
        raw_full = [sem(f"raw_full_{s}") for s in range(RING_SLOTS)]
        hi_made = sem("hi_made")
        lo_made = sem("lo_made")
        ring_free = sem("ring_free")
        row_sq = [sem(f"row_squares_{s}") for s in range(3)]
        var_made = [sem(f"variance_{s}") for s in range(3)]
        rooted = [sem(f"rooted_{s}") for s in range(3)]
        inverted = [sem(f"inverted_{s}") for s in range(3)]
        normed = [sem(f"rows_normed_{s}") for s in range(3)]
        turned = [sem(f"turned_{s}") for s in range(3)]
        t_hi = [sem(f"turned_hi_{s}") for s in range(3)]
        t_lo = [sem(f"turned_lo_{s}") for s in range(3)]
        proj_out = sem("proj_copied_out")
        squared = sem("proj_squared")
        reduced = sem("proj_squares_reduced")
        st_var, st_root, st_inv = sem("stats_var"), sem("stats_rooted"), sem("stats_inverted")
        s_sgp = sem("gmlp_params_loaded")
        s_sgm = sem("gmlp_masked")
        vb_made, mixed, gated = sem("vb_made"), sem("mixed"), sem("gated")
        qk_normed, v_copied = sem("qk_normed"), sem("v_copied")
        qk_turned, qkT_out = sem("qk_turned"), sem("qkT_out")
        z_done, z_abs, z_exp, z_ln = sem("z_done"), sem("z_abs"), sem("z_exp"), sem("z_ln")
        sp_made, sp_kept = sem("sp_made"), sem("sp_kept")
        tails, z_blocked, w_made = sem("tails"), sem("z_blocked"), sem("w_made")
        pv_done, y_out = sem("pv_done"), sem("y_out")
        s_x1 = sem("x1_loaded")
        out_added = sem("out_added")
        q_out, q_sq, q_pair = sem("q_out"), sem("q_squared"), sem("q_pair_added")
        q_ss, q_var, q_root, q_inv = sem("q_ss"), sem("q_var"), sem("q_root"), sem("q_inv")
        s_done, s_out, topk, sm_sub, sm_exp = (sem("scores_done"), sem("scores_out"), sem("topk_step"),
                                               sem("softmax_sub"), sem("softmax_exp"))
        sel_made, sel_turned, selT_out = sem("sel_made"), sem("sel_turned"), sem("selT_out")
        hot_made, g_mm, g_out, g_stored = sem("hot_made"), sem("g_mm"), sem("g_out"), sem("g_stored")
        g_loaded = [sem(f"gate_loaded_{c}") for c in range(GROUP)]
        gelu_made, act_made, ahi_made, alo_made = (sem("gelu_made"), sem("act_made"), sem("a_hi_made"), sem("a_lo_made"))
        y_mm, y_added = sem("expert_y"), sem("expert_y_added")
        s_stored = sem("out_stored")

        block = ctx.enter_context(nc.Block())

        def turned_from(stage, tt, k):
            if stage == IN_NORM:
                return x0[:, tt, k * P:(k + 1) * P]
            if stage == FFN_NORM:
                return x1n[:, tt, k * P:(k + 1) * P]
            part, k = (Q_PART, k) if k < HEADS else (U_PART, k - HEADS)
            return proj[:, part, tt, k * P:(k + 1) * P]

        def bcast(ap, shape, *axes):
            for a in axes:
                ap = ap.unsqueeze(a)
            return ap.broadcast_to(shape)

        @block.sync
        def _(sp_eng):
            for t in range(TT):
                sp_eng.dma_start(x0[:, t, :], x[t * P:(t + 1) * P, :]).then_inc(s_x[t], 16)

            def load(src, p, slot, n):
                sp_eng.wait_ge(lo_made, p - 1)
                sp_eng.dma_start(raw[:, slot, :], src[bass.ds(n, 1)].rearrange("a p n -> p (a n)"))\
                      .then_inc(raw_full[slot], 16)

            for p in range(RING_SLOTS):
                sp_eng.dma_start(raw[:, p, :], w_in[p]).then_inc(raw_full[p], 16)
            with sp_eng.Fori(1, IN_PIECES // 2) as i:
                for s in range(2):
                    load(w_in, 2 * i + s, s, 2 * i + s)
            for src, first in ((w_out, P_OUT), (w_q, P_QUERY)):
                with sp_eng.Fori(0, MM_PIECES // 2) as i:
                    for s in range(2):
                        load(src, 2 * i + s + first, s, 2 * i + s)
            g_view = gates.rearrange("i j t -> j i t")
            for t in range(TT):
                sp_eng.wait_ge(g_out, (t + 1) * (P // 4) + 4)
                sp_eng.dma_start(g_view[:, :, t * P:(t + 1) * P], gbuf[:]).then_inc(g_stored, 16)
            sp_eng.wait_ge(g_stored, 16 * TT)

            def load_gate(i, c):
                sp_eng.dma_start(gch[:, c, :], gates[bass.ds(i, 1)].rearrange("a j t -> j (a t)"))\
                      .then_inc(g_loaded[c], 16)

            for c in range(GROUP):
                load_gate(c, c)
                load(pu, P_PEER + c, c % 2, c)
            with sp_eng.Fori(1, N_GROUPS) as g:
                for c in range(GROUP):
                    sp_eng.wait_ge(act_made, GROUP * g + c - 3)
                    load_gate(GROUP * g + c, c)
                    p = 8 * g + 2 * c + (P_PEER - GROUP)
                    load(pu, p, 0, GROUP * g + c)
                    load(pv, p + 1, 1, GROUP * g + c - GROUP)
            for c in range(GROUP):
                load(pv, P_PEER + GROUP + 8 * (N_GROUPS - 1) + c, c % 2, GROUP * (N_GROUPS - 1) + c)
            sp_eng.wait_ge(y_added, 16 * N_GROUPS + 4)
            for t in range(TT):
                sp_eng.dma_start(out[t * P:(t + 1) * P, :], x1[:, t, :]).then_inc(s_stored, 16)
            sp_eng.wait_ge(s_stored, 16 * TT)

        @block.gpsimd
        def _(pool):
            made = [0]

            def const(ins):
                made[0] += 1
                ins.then_inc(s_const, 1)
                pool.wait_ge(s_const, made[0])

            for dst, src in ((gains[:, 0, :], nm), (gains[:, 1, :], ny), (gains[:, 2, :], nf), (qgain, qn),
                             (kgain, kn), (sgb_s, sgb), (keysT[:], keys)):
                pool.dma_start(dst, src).then_inc(s_par, 16)
            const(pool.memset(ident[:], 0.0))
            const(pool.affine_select(out=ident[:], in_=ident[:], compare_op=ALU.not_equal, fill=1.0, base=0,
                                     pattern=[[-1, P]], channel_multiplier=1))
            const(pool.memset(neg1[:], -1.0))
            const(pool.affine_select(out=tri[:], in_=neg1[:], compare_op=ALU.is_ge, fill=0.0, base=0,
                                     pattern=[[-1, P]], channel_multiplier=1))
            const(pool.memset(keep[:], 1.0))
            const(pool.affine_select(out=keep[:], in_=keep[:], compare_op=ALU.is_gt, fill=0.0, base=0,
                                     pattern=[[1, P]], channel_multiplier=-1))
            const(pool.memset(block_m[:], 0.0))
            const(pool.affine_select(out=block_m[:], in_=block_m[:], compare_op=ALU.is_gt, fill=-BIG, base=0,
                                     pattern=[[1, P]], channel_multiplier=-1))
            const(pool.iota(iota[:], [[1, NK]], base=0, channel_multiplier=0,
                            allow_small_or_imprecise_dtypes=True))
            const(pool.iota(iota16[:], [[1, TOPK]], base=0, channel_multiplier=0,
                            allow_small_or_imprecise_dtypes=True))
            pool.wait_ge(ring_free, RING_SLOTS + IN_PIECES)
            pool.dma_start(sgw_s[:], sgw).then_inc(s_sgp, 16)
            pool.dma_start(sgn_s[:], sgn).then_inc(s_sgp, 16)
            for i in range(HEADS // 2):
                if i:
                    pool.wait_ge(pv_done, 2 * i)
                for ab in range(2):
                    pool.wait_ge(proj_out, 4 * IN_CHUNKS)
                    pool.tensor_copy(v_h[:, ab, :, :], proj[:, V_PART, :, bass.ds((2 * i + ab) * HD, HD)])\
                        .then_inc(v_copied, 1)
            pool.wait_ge(pv_done, HEADS)
            pool.wait_ge(v_copied, HEADS)
            pool.dma_start(x1[:], x.rearrange("(t p) d -> p t d", p=P)).then_inc(s_x1, 16)

        @block.scalar
        def _(act):
            def make_hi(p, slot, use):
                act.wait_ge(raw_full[slot], 16 * use)
                act.wait_ge(ring_free, p + 1)
                act.activation(hi[:, slot, :], raw[:, slot, :], ACT.Copy).then_inc(hi_made, 1)

            def root(stage, cols):
                act.wait_ge(var_made[stage], 1)
                act.activation(ss[:, 0:cols], ss[:, 0:cols], ACT.Sqrt).then_inc(rooted[stage], 1)

            def turn_hi(stage):
                for k in range(KD):
                    act.wait_ge(turned[stage], k + 1)
                    act.activation(actT_hi[:, k, :], ps[:, k % NBANK, :], ACT.Copy,
                                   scale=gains[:, stage, k:k + 1]).then_inc(t_hi[stage], 1)

            for t in range(TT):
                act.wait_ge(s_x[t], 16)
                act.activation(junk0[:], x0[:, t, :], ACT.Square, accum_out=ss[:, t:t + 1])\
                   .then_inc(row_sq[IN_NORM], 1)
                act.wait_ge(row_sq[IN_NORM], t + 1)
            root(IN_NORM, TT)
            act.wait_ge(s_par, 16 * 7)
            turn_hi(IN_NORM)

            def evac_in(c, i, part, cc, func):
                act.wait_ge(ring_free, 4 * c + (4 + RING_SLOTS))
                for t in range(TT):
                    dst = proj[:, bass.ds(part, 1), t, cc * BANK:(cc + 1) * BANK].rearrange("p a n -> p (a n)")
                    act.activation(dst, ps[:, cc * 4 + t, :], func).then_inc(proj_out, 1)
                    act.wait_ge(proj_out, 4 * c + t + 1)
                    act.wait_ge(reduced, 4 * c + t + 1)
                    act.activation(sq[:, t % 2, :], dst, ACT.Square).then_inc(squared, 1)

            act.sem_inc(reduced, 2)
            act.wait_ge(raw_full[0], 16)
            make_hi(0, 0, 1)
            for first, count, func in ((0, 3, ACT.Copy), (3, 2, ACT.Gelu)):
                for i in range(first, first + count):
                    for cc in range(2):
                        for kq in range(KQ):
                            n = 4 * cc + kq + 1
                            make_hi(8 * i + n, n % 2, 4 * i + n // 2 + 1)
                        evac_in(2 * i + cc, i, i, cc, func)
            act.wait_ge(st_var, 1)
            st = stats[:].rearrange("p a t h -> p (a t h)")
            act.activation(st, st, ACT.Sqrt).then_inc(st_root, 1)

            for i in range(HEADS // 2):
                for ab in range(2):
                    n = 2 * i + ab
                    for j, gain in ((0, qgain), (1, kgain)):
                        act.wait_ge(qk_turned, 2 * n + j + 1)
                        act.activation(qkT[:, ab, j, :], ps[:, 7 * j, :], ACT.Copy, scale=gain)\
                           .then_inc(qkT_out, 1)
                for ab in range(2):
                    n = 2 * i + ab
                    z = ps[:, 1 + 3 * ab:4 + 3 * ab, :].rearrange("p b n -> p (b n)")[:, 0:1280]
                    act.wait_ge(z_done, n + 1)
                    act.activation(sp_t[:, ab, :], z, ACT.Abs).then_inc(z_abs, 1)
                    act.wait_ge(z_abs, n + 1)
                    act.activation(sp_t[:, ab, :], sp_t[:, ab, :], ACT.Exp, scale=-1.0).then_inc(z_exp, 1)
                    act.wait_ge(z_exp, n + 1)
                    act.activation(sp_t[:, ab, :], sp_t[:, ab, :], ACT.Ln, bias=1.0).then_inc(z_ln, 1)
                for ab in range(2):
                    n = 2 * i + ab
                    z = ps[:, 1 + 3 * ab:4 + 3 * ab, :].rearrange("p b n -> p (b n)")[:, 0:1280]
                    act.wait_ge(z_blocked, 2 * n + 2)
                    act.activation(w_att[:, ab, :], z, ACT.Exp).then_inc(w_made, 1)
                for ab in range(2):
                    n = 2 * i + ab
                    act.wait_ge(pv_done, n + 1)
                    act.activation(proj[:, Q_PART, :, bass.ds(n * HD, HD)],
                                   ps[:, 7 * ab, :].rearrange("p (t c) -> p t c", t=TT), ACT.Copy)\
                       .then_inc(y_out, 1)

            act.wait_ge(y_out, HEADS + 1)
            act.wait_ge(gated, HEADS)
            n = 0
            for j, part in enumerate((Q_PART, U_PART)):
                for t in range(TT):
                    act.activation(junk1[:, 0:WIDTH], proj[:, part, t, :], ACT.Square,
                                   accum_out=ss[:, j * TT + t:j * TT + t + 1]).then_inc(row_sq[MIX_NORM], 1)
                    n += 1
                    act.wait_ge(row_sq[MIX_NORM], n)
            root(MIX_NORM, 2 * TT)
            turn_hi(MIX_NORM)
            with act.Fori(0, MM_PIECES // 2) as i:
                for s in range(2):
                    make_hi(2 * i + (P_OUT + 1 + s), (1 + s) % 2, i + (P_OUT // 2 + 1 + s))
            for t in range(TT):
                act.wait_ge(out_added, 8 + 16)
                act.activation(junk2[:], x1[:, t, :], ACT.Square, accum_out=ss[:, t:t + 1])\
                   .then_inc(row_sq[FFN_NORM], 1)
                act.wait_ge(row_sq[FFN_NORM], t + 1)
            root(FFN_NORM, TT)
            turn_hi(FFN_NORM)

            for c in range(4):
                for kq in range(KQ):
                    m = 4 * c + kq + 1
                    if m < MM_PIECES:
                        make_hi(P_QUERY + m, m % 2, (P_QUERY + m) // 2 + 1)
                act.wait_ge(ring_free, P_QUERY + 4 * c + 4 + RING_SLOTS)
                for b in range(4):
                    m = 4 * c + b
                    act.activation(qT[:, m, :], ps[:, (c % 2) * 4 + b, :], ACT.Copy).then_inc(q_out, 1)
                    if m >= 2:
                        act.wait_ge(q_pair, m // 2)
                    act.activation(sq[:, b % 2, :], ps[:, (c % 2) * 4 + b, :], ACT.Square).then_inc(q_sq, 1)
            act.wait_ge(q_var, 1)
            act.activation(rq, rq, ACT.Sqrt).then_inc(q_root, 1)
            with act.Fori(0, TT) as t:
                act.wait_ge(sm_sub, t + 1)
                act.activation(gate_e[:], gate_e[:], ACT.Exp).then_inc(sm_exp, 1)

            waited = act.alloc_register("waited")
            for t in range(TT):
                if t:
                    act.wait_ge(g_stored, 16 * t)
                with act.Fori(0, P // 16) as b:
                    for j in range(4):
                        act.wait_ge(g_mm, 32 * t + 4 * b + (j + 1) + 4)
                        act.reg_mov(waited, 0)
                        act.activation(gbuf[:, :, bass.ds(16 * b + 4 * j, 4)],
                                       ps[:, j, :].rearrange("p (t i) -> p i t", t=4), ACT.Copy)\
                           .then_inc(g_out, 1)

            def expert_act(p, i, z_bank, par, c):
                act.wait_ge(ring_free, p + (1 + RING_SLOTS))
                act.activation(gelu[:, z_bank, :], ps[:, z_bank, :], ACT.Gelu).then_inc(gelu_made, 1)
                act.wait_ge(act_made, i + 1)
                act.activation(a_hi[:, par, c, :], act_f[:, z_bank, :], ACT.Copy).then_inc(ahi_made, 1)

            make_hi(P_PEER, 0, P_PEER // 2 + 1)
            for c in range(GROUP):
                m = P_PEER + c + 1
                make_hi(m, m % 2, m // 2 + 1)
                expert_act(P_PEER + c, c, c % 2, 0, c)

            def group(g, par):
                for c in range(GROUP):
                    p = 8 * g + (2 * c + P_PEER - GROUP)
                    use = 4 * g + (c + (P_PEER - GROUP) // 2 + 1)
                    make_hi(p + 1, 1, use)
                    make_hi(p + 2, 0, use + 1)
                    expert_act(p, 4 * g + c, c % 2, par, c)

            with act.Fori(0, (N_GROUPS - 2) // 2) as r:
                group(2 * r + 1, 1)
                group(2 * r + 2, 0)
            group(N_GROUPS - 1, 1)
            for c in range(1, GROUP):
                m = P_PEER + 2 * N_GROUPS * GROUP - GROUP + c
                make_hi(m, m % 2, m // 2 + 1)

        @block.vector
        def _(dve):
            def make_lo(p, slot):
                dve.wait_ge(hi_made, p + 1)
                dve.tensor_tensor(lo[:, slot, :], raw[:, slot, :], hi[:, slot, :].bitcast(F32), ALU.subtract)\
                   .then_inc(lo_made, 1)

            def inverse_rms(stage, cols, width, n_sq):
                dve.wait_ge(row_sq[stage], n_sq)
                dve.tensor_scalar(ss[:, 0:cols], ss[:, 0:cols], 1.0 / width, EPS, ALU.mult, ALU.add)\
                   .then_inc(var_made[stage], 1)
                dve.wait_ge(rooted[stage], 1)
                dve.reciprocal(ss[:, 0:cols], ss[:, 0:cols]).then_inc(inverted[stage], 1)
                dve.wait_ge(inverted[stage], 1)

            def turn_lo(stage):
                for k in range(KD):
                    dve.wait_ge(t_hi[stage], k + 1)
                    dve.scalar_tensor_tensor(out=actT_lo[:, k, :], in0=ps[:, k % NBANK, :],
                                             scalar=gains[:, stage, k:k + 1], in1=actT_hi[:, k, :].bitcast(F32),
                                             op0=ALU.mult, op1=ALU.subtract).then_inc(t_lo[stage], 1)

            inverse_rms(IN_NORM, TT, D, TT)
            for t in range(TT):
                dve.tensor_scalar(x0[:, t, :], x0[:, t, :], ss[:, t:t + 1], None, ALU.mult)\
                   .then_inc(normed[IN_NORM], 1)
            dve.wait_ge(s_par, 16 * 7)
            turn_lo(IN_NORM)

            def sum_squares(c, part, cc):
                for t in range(TT):
                    dve.wait_ge(squared, 4 * c + (t + 1 + 8))
                    dve.tensor_reduce(stats[:, bass.ds(part, 1), t, 4 * cc:4 * cc + 4].rearrange("p a h -> p (a h)"),
                                      sq[:, t % 2, :].rearrange("p (h c) -> p h c", c=HD), AX_X, ALU.add)\
                       .then_inc(reduced, 1)

            make_lo(0, 0)
            with dve.Fori(0, PARTS) as i:
                for cc in range(2):
                    for kq in range(KQ):
                        n = 4 * cc + kq + 1
                        make_lo(8 * i + n, n % 2)
                    sum_squares(2 * i + cc, i, cc)
            st = stats[:].rearrange("p a t h -> p (a t h)")
            dve.wait_ge(reduced, 4 * IN_CHUNKS + 2)
            dve.tensor_scalar(st, st, 1.0 / HD, EPS, ALU.mult, ALU.add).then_inc(st_var, 1)
            dve.tensor_scalar(qgain, qgain, SCALE, None, ALU.mult).then_inc(st_inv, 1)
            dve.wait_ge(st_root, 1)
            dve.reciprocal(st, st).then_inc(st_inv, 1)
            dve.wait_ge(st_inv, 2)

            dve.wait_ge(s_sgp, 32)
            dve.memset(sgw_s[64:128, :, 0:64], 0.0).then_inc(s_sgm, 1)
            for h in range(HEADS):
                cols = slice(h * HD, (h + 1) * HD)
                for t in range(TT):
                    dve.scalar_tensor_tensor(out=proj[:, G_PART, t, cols], in0=proj[:, G_PART, t, cols],
                                             scalar=stats[:, G_PART, t, h:h + 1], in1=sgn_s[:, cols],
                                             op0=ALU.mult, op1=ALU.mult).then_inc(vb_made, 1)
            for h in range(HEADS):
                cols = slice(h * HD, (h + 1) * HD)
                dve.wait_ge(mixed, h + 1)
                dve.scalar_tensor_tensor(out=proj[:, U_PART, :, cols],
                                         in0=ps[:, h, :].rearrange("p (t c) -> p t c", t=TT),
                                         scalar=sgb_s[:, h:h + 1], in1=proj[:, U_PART, :, cols],
                                         op0=ALU.add, op1=ALU.mult).then_inc(gated, 1)

            with dve.Fori(0, HEADS // 2) as i:
                for ab in range(2):
                    n = 2 * i + ab
                    for j in range(2):
                        r = stats[:, j, :, bass.ds(n, 1)]
                        dve.tensor_tensor(qk_n[:, ab, j, :, :], proj[:, j, :, bass.ds(n * HD, HD)],
                                          r.broadcast_to([P, TT, HD]), ALU.mult).then_inc(qk_normed, 1)
                for ab in range(2):
                    n = 2 * i + ab
                    z = ps[:, 1 + 3 * ab:4 + 3 * ab, :].rearrange("p b n -> p (b n)")
                    dve.wait_ge(z_ln, n + 1)
                    dve.scalar_tensor_tensor(out=sp[:, ab, :], in0=z[:, 0:1280], scalar=0.0, in1=sp_t[:, ab, :],
                                             op0=ALU.max, op1=ALU.add).then_inc(sp_made, 1)
                    dve.wait_ge(sp_made, n + 1)
                    three = sp[:, ab, 0:1280].rearrange("p (b n) -> p b n", n=256)[:, 0:5:2, 0:P]
                    dve.tensor_tensor(three, three, bcast(keep[:], [P, 3, P], 1), ALU.mult).then_inc(sp_kept, 1)
                    dve.tensor_tensor(sp[:, ab, 896:1024], sp[:, ab, 896:1024], keep[:], ALU.mult)\
                       .then_inc(sp_kept, 1)
                for ab in range(2):
                    n = 2 * i + ab
                    z = ps[:, 1 + 3 * ab:4 + 3 * ab, :]
                    dve.wait_ge(tails, n + 1)
                    dve.tensor_tensor(z[:, :, 0:P], z[:, :, 0:P], bcast(block_m[:], [P, 3, P], 1), ALU.add)\
                       .then_inc(z_blocked, 1)
                    dve.tensor_tensor(z[:, 1, 384:512], z[:, 1, 384:512], block_m[:], ALU.add)\
                       .then_inc(z_blocked, 1)

            inverse_rms(MIX_NORM, 2 * TT, WIDTH, 2 * TT)
            for j, part in enumerate((Q_PART, U_PART)):
                for t in range(TT):
                    dve.tensor_scalar(proj[:, part, t, :], proj[:, part, t, :], ss[:, j * TT + t:j * TT + t + 1],
                                      None, ALU.mult).then_inc(normed[MIX_NORM], 1)
            turn_lo(MIX_NORM)
            dve.wait_ge(s_x1, 16)
            with dve.Fori(0, 2) as i:
                for cc in range(2):
                    for kq in range(KQ):
                        n = 4 * cc + kq + 1
                        make_lo(8 * i + (P_OUT + n), n % 2)
                    dve.wait_ge(ring_free, 8 * i + (P_OUT + 4 * cc + 4 + RING_SLOTS))
                    for t in range(TT):
                        col = x1[:, t, bass.ds(i * 2 * BANK + cc * BANK, BANK)]
                        dve.tensor_tensor(col, ps[:, cc * 4 + t, :], col, ALU.add).then_inc(out_added, 1)
            inverse_rms(FFN_NORM, TT, D, TT)
            for t in range(TT):
                dve.tensor_scalar(x1n[:, t, :], x1[:, t, :], ss[:, t:t + 1], None, ALU.mult)\
                   .then_inc(normed[FFN_NORM], 1)
            turn_lo(FFN_NORM)

            for c in range(4):
                for kq in range(KQ):
                    m = 4 * c + kq + 1
                    if m < MM_PIECES:
                        make_lo(P_QUERY + m, m % 2)
                for h in range(2 * c, 2 * c + 2):
                    dve.wait_ge(q_sq, 2 * h + 2)
                    dve.tensor_tensor(sqh[:, h, :], sq[:, 0, :], sq[:, 1, :], ALU.add).then_inc(q_pair, 1)
            dve.wait_ge(q_ss, 1)
            dve.tensor_scalar(rq, ps[:, 0, 0:TT * PH].rearrange("p (t h) -> p t h", t=TT), -1.0 / (2 * HD), EPS,
                              ALU.mult, ALU.add).then_inc(q_var, 1)
            dve.wait_ge(q_root, 1)
            dve.reciprocal(rq, rq).then_inc(q_inv, 1)
            dve.wait_ge(q_inv, 1)

            STEPS = 22
            with dve.Fori(0, TT) as t:
                step = [0]

                def done(ins):
                    step[0] += 1
                    ins.then_inc(topk, 1)
                    dve.wait_ge(topk, STEPS * t + step[0])

                def carry():
                    dve.memset(tick, 0.0)

                def top16(count, values, best, places):
                    for half in range(2):
                        eight = slice(8 * half, 8 * half + 8)
                        carry()
                        for n in range(count):
                            last = dve.max(best(n)[:, eight], values(n))
                        done(last)
                        carry()
                        for n in range(count):
                            last = dve.max_index(places(n)[:, eight], best(n)[:, eight], values(n))
                        done(last)
                        if not half:
                            carry()
                            for n in range(count):
                                last = dve.match_replace(values(n), best(n)[:, eight], values(n), NEG)
                            done(last)

                dve.wait_ge(s_done, t + 1)
                r = rq[:, bass.ds(t, 1), :].rearrange("p a h -> p (a h)")
                dve.tensor_tensor(s_sb[:].rearrange("p (h two) n -> p h (two n)", two=2),
                                  ps[:, 0:4, :].rearrange("p b (h n) -> p (b h) n", h=2),
                                  bcast(r, [P, PH, 2 * NK], 2), ALU.mult).then_inc(s_out, 1)
                dve.wait_ge(s_out, t + 1)
                top16(2 * PH, lambda n: s_sb[:, n, :], lambda n: v12[:, n, :], lambda n: i12u[:, n, :])
                v = v12[:].rearrange("p (h two) k -> p h two k", two=2)
                shape = [P, PH, TOPK, TOPK]
                done(dve.tensor_tensor(cand[:], bcast(v[:, :, 0, :], shape, 3), bcast(v[:, :, 1, :], shape, 2), ALU.add))
                flat = cand[:].rearrange("p h a b -> p h (a b)")
                top16(PH, lambda n: flat[:, n, :], lambda n: tv[:, n, :], lambda n: tpos[:, n, :])
                done(dve.tensor_tensor(gate_e[:], tv[:], tv[:, :, 0:1].broadcast_to([P, PH, TOPK]), ALU.subtract))
                step_sub = dve.tensor_copy(i12f[:], i12u[:])
                step_sub.then_inc(sm_sub, 1)
                pos = tpos[:].rearrange("p h k -> p (h k)")
                dve.tensor_scalar(posu[:, 0, :], pos, 4, None, ALU.logical_shift_right)
                done(dve.tensor_scalar(posu[:, 1, :], pos, 15, None, ALU.bitwise_and))
                done(dve.tensor_copy(posf[:], posu[:]))
                full = [P, PH * TOPK, TOPK]
                idx = i12f[:].rearrange("p (h two) a -> p h two a", two=2)
                eq4 = eq[:].rearrange("p (h k) a -> p h k a", h=PH)
                for j in range(2):
                    done(dve.tensor_tensor(eq[:], bcast(iota16[:], full, 1), bcast(posf[:, j, :], full, 2),
                                           ALU.is_equal))
                    done(dve.tensor_tensor(eq4, eq4, bcast(idx[:, :, j, :], [P, PH, TOPK, TOPK], 2), ALU.mult))
                    done(dve.tensor_reduce(sel[:, j, :], eq[:], AX_X, ALU.add))
                dve.wait_ge(sm_exp, t + 1)
                done(dve.tensor_reduce(gate_s[:, 0, :], gate_e[:], AX_X, ALU.add))
                done(dve.reciprocal(gate_s[:, 1, :], gate_s[:, 0, :]))
                dve.tensor_tensor(sel[:, 2, :].rearrange("p (h k) -> p h k", h=PH), gate_e[:],
                                  bcast(gate_s[:, 1, :], [P, PH, TOPK], 2), ALU.mult).then_inc(sel_made, 1)
                dve.wait_ge(sel_turned, t + 1)
                dve.tensor_copy(selT[:, :, bass.ds(t * P, P)],
                                ps[:, 4, 0:3 * P].rearrange("p (s n) -> p s n", s=3)).then_inc(selT_out, 1)
                assert step[0] == STEPS, step[0]
            dve.wait_ge(selT_out, TT)

            with dve.Fori(0, SEQ // 16) as b:
                for j in range(4):
                    dve.wait_ge(g_mm, 4 * b + (j + 1))
                    for q in range(4):
                        m = 4 * j + q
                        tok = bass.ds(16 * b + m, 1)
                        dve.tensor_scalar(hot_a[:, m, :], iota[:], selT[:, 0, tok], selT[:, 2, tok],
                                          ALU.is_equal, ALU.mult)
                        last = dve.tensor_scalar(hot_b[:, m, :], iota[:], selT[:, 1, tok], None, ALU.is_equal)
                    last.then_inc(hot_made, 1)

            def expert_act_dve(i, z_bank, par, c, use):
                dve.wait_ge(gelu_made, i + 1)
                dve.wait_ge(g_loaded[c], 16 * use)
                dve.tensor_tensor(act_f[:, z_bank, :], gelu[:, z_bank, :], gch[:, c, :], ALU.mult)\
                   .then_inc(act_made, 1)
                dve.wait_ge(ahi_made, i + 1)
                dve.tensor_tensor(a_lo[:, par, c, :], act_f[:, z_bank, :], a_hi[:, par, c, :].bitcast(F32),
                                  ALU.subtract).then_inc(alo_made, 1)

            def add_out(p, g_before, c):
                for u in range(2):
                    if u:
                        dve.wait_ge(ring_free, p + (1 + RING_SLOTS))
                    else:
                        dve.wait_ge(y_mm, 4 * g_before + (c + 1))
                    for t in range(2):
                        col = x1[:, 2 * u + t, c * BANK:(c + 1) * BANK]
                        dve.tensor_tensor(col, ps[:, 4 + 2 * u + t, :], col, ALU.add).then_inc(y_added, 1)

            make_lo(P_PEER, 0)
            for c in range(GROUP):
                make_lo(P_PEER + c + 1, (c + 1) % 2)
                expert_act_dve(c, c % 2, 0, c, 1)

            def group(g, par):
                for c in range(GROUP):
                    p = 8 * g + (2 * c + P_PEER - GROUP)
                    make_lo(p + 1, 1)
                    make_lo(p + 2, 0)
                    expert_act_dve(4 * g + c, c % 2, par, c, g + 1)
                    add_out(p + 1, g - 1, c)

            with dve.Fori(0, (N_GROUPS - 2) // 2) as r:
                group(2 * r + 1, 1)
                group(2 * r + 2, 0)
            group(N_GROUPS - 1, 1)
            for c in range(GROUP):
                m = P_PEER + 2 * N_GROUPS * GROUP - GROUP + c
                if c:
                    make_lo(m, m % 2)
                add_out(m, N_GROUPS - 1, c)

        @block.tensor
        def _(pe):
            def three(dst, w_h, w_l, m_h, m_l, first, last):
                pe.matmul(dst, w_h, m_h, start=first, stop=False)
                pe.matmul(dst, w_h, m_l, start=False, stop=False)
                return pe.matmul(dst, w_l, m_h, start=False, stop=last)

            def turn(stage, sources):
                pe.wait_ge(normed[stage], sources)
                for k in range(KD):
                    if k >= NBANK:
                        pe.wait_ge(t_lo[stage], k - NBANK + 1)
                    for t in range(TT):
                        last = pe.transpose(ps[:, k % NBANK, t * P:(t + 1) * P], turned_from(stage, t, k), ident[:])
                    last.then_inc(turned[stage], 1)
                pe.wait_ge(t_lo[stage], KD)

            def rows_piece(p, slot, kq, bank):
                pe.wait_ge(lo_made, p + 1)
                for kk in range(4):
                    k = 4 * kq + kk
                    cols = slice(kk * BANK, (kk + 1) * BANK)
                    for t in range(TT):
                        a = slice(t * P, (t + 1) * P)
                        last = three(ps[:, bank + t, :], actT_hi[:, k, a], actT_lo[:, k, a],
                                     hi[:, slot, cols], lo[:, slot, cols], k == 0, k == KD - 1)
                last.then_inc(ring_free, 1)
                return last

            pe.sem_inc(ring_free, RING_SLOTS)
            pe.sem_inc(squared, 8)
            pe.wait_ge(s_const, 10)
            turn(IN_NORM, TT)
            with pe.Fori(0, PARTS) as i:
                for cc in range(2):
                    pe.wait_ge(squared, 8 * i + (4 * cc + 4))
                    for kq in range(KQ):
                        rows_piece(8 * i + (4 * cc + kq), kq % 2, kq, 4 * cc)

            pe.wait_ge(s_sgm, 1)
            pe.wait_ge(squared, 8 + 4 * IN_CHUNKS)
            for h in range(HEADS):
                pe.wait_ge(vb_made, TT * (h + 1))
                pe.matmul(ps[:, h, :], sgw_s[:, h, :], proj[:, G_PART, :, h * HD:(h + 1) * HD],
                          start=True, stop=True).then_inc(mixed, 1)

            Z_AT = ((0, 0), (1, 0), (2, 0), (1, 384))
            pe.wait_ge(gated, HEADS)
            pe.sem_inc(y_out, 1)
            with pe.Fori(0, HEADS // 2) as i:
                pe.wait_ge(y_out, 2 * i + 1)
                for ab in range(2):
                    n = 2 * i + ab
                    for j in range(2):
                        pe.wait_ge(qk_normed, 2 * n + (j + 1))
                        if ab:
                            pe.wait_ge(qkT_out, 4 * i + (j + 1))
                        for t in range(TT):
                            last = pe.transpose(ps[:, 7 * j, t * P:(t + 1) * P], qk_n[:, ab, j, t, :], ident[:])
                        last.then_inc(qk_turned, 1)
                for ab in range(2):
                    n = 2 * i + ab
                    pe.wait_ge(qkT_out, 2 * n + 2)
                    for b in range(TT):
                        bank, col = Z_AT[b]
                        last = pe.matmul(ps[:, 1 + 3 * ab + bank, col:col + SEQ - b * P],
                                         qkT[:, ab, 1, b * P:(b + 1) * P], qkT[:, ab, 0, b * P:SEQ],
                                         start=(b < 3), stop=True, skip_group_check=True)
                    last.then_inc(z_done, 1)
                for ab in range(2):
                    n = 2 * i + ab
                    pe.wait_ge(sp_kept, 2 * n + 2)
                    for b in range(TT):
                        bank, col = Z_AT[b]
                        for b2 in range(b, TT):
                            bank2, col2 = Z_AT[b2]
                            width = SEQ - b2 * P
                            at2 = bank2 * BANK + col2
                            off = col + (b2 - b) * P
                            last = pe.matmul(ps[:, 1 + 3 * ab + bank, off:off + width],
                                             tri[:] if b2 == b else neg1[:], sp[:, ab, at2:at2 + width],
                                             start=False, stop=True, skip_group_check=True)
                    last.then_inc(tails, 1)
                for ab in range(2):
                    n = 2 * i + ab
                    pe.wait_ge(w_made, n + 1)
                    pe.wait_ge(v_copied, n + 1)
                    if not ab:
                        pe.wait_ge(qkT_out, 4 * i + 4)
                    for t in range(TT):
                        for b in range(t + 1):
                            bank, col = Z_AT[b]
                            at1 = bank * BANK + col + (t - b) * P
                            last = pe.matmul(ps[:, 7 * ab, t * P:(t + 1) * P], w_att[:, ab, at1:at1 + P],
                                             v_h[:, ab, b, :], start=(t == 0 and b == 0), stop=(b == t),
                                             skip_group_check=True)
                    last.then_inc(pv_done, 1)

            turn(MIX_NORM, 2 * TT)
            pe.sem_inc(out_added, 8)
            with pe.Fori(0, 2) as i:
                for cc in range(2):
                    pe.wait_ge(out_added, 8 * i + (4 * cc + 4))
                    for kq in range(KQ):
                        rows_piece(8 * i + (P_OUT + 4 * cc + kq), kq % 2, kq, 4 * cc)
            turn(FFN_NORM, TT)

            for c in range(4):
                if c >= 2:
                    pe.wait_ge(q_out, 4 * (c - 1))
                    pe.wait_ge(q_sq, 4 * (c - 1))
                for kq in range(KQ):
                    m = 4 * c + kq
                    pe.wait_ge(lo_made, P_QUERY + m + 1)
                    for kk in range(4):
                        k = 4 * kq + kk
                        for b in range(4):
                            col = slice(kk * BANK + b * P, kk * BANK + (b + 1) * P)
                            last = three(ps[:, 4 * (c % 2) + b, :], hi[:, m % 2, col], lo[:, m % 2, col],
                                         actT_hi[:, k, :], actT_lo[:, k, :], k == 0, k == KD - 1)
                    last.then_inc(ring_free, 1)
            pe.wait_ge(q_pair, PH)
            pe.wait_ge(q_out, 16)
            for t in range(TT):
                for h in range(PH):
                    col = t * PH + h
                    last = pe.matmul(ps[:, 0, col:col + 1], sqh[:, h, t * P:(t + 1) * P], neg1[:, 0:1],
                                     start=True, stop=True)
            last.then_inc(q_ss, 1)
            pe.wait_ge(q_var, 1)
            for t in range(TT):
                pe.wait_ge(s_out, t)
                for m in range(2 * PH):
                    last = pe.matmul(ps[:, m // 4, (m % 4) * NK:(m % 4 + 1) * NK], qT[:, m, t * P:(t + 1) * P],
                                     keysT[:, m % 2, :], start=True, stop=True)
                last.then_inc(s_done, 1)
                pe.wait_ge(sel_made, t + 1)
                pe.wait_ge(selT_out, t)
                for j in range(3):
                    last = pe.transpose(ps[:, 4, j * P:(j + 1) * P], sel[:, j, :], ident[:])
                last.then_inc(sel_turned, 1)
            pe.sem_inc(g_mm, 4)
            pe.sem_inc(g_out, 4)
            pe.wait_ge(s_out, TT)
            with pe.Fori(0, SEQ // 16) as b:
                for j in range(4):
                    pe.wait_ge(hot_made, 4 * b + (j + 1))
                    pe.wait_ge(g_out, 4 * b + (j + 1))
                    for q in range(4):
                        m = 4 * j + q
                        last = pe.matmul(ps[:, j, q * NK:(q + 1) * NK], hot_b[:, m, :], hot_a[:, m, :],
                                         start=True, stop=True)
                    last.then_inc(g_mm, 1)
            pe.wait_ge(g_out, 4 + SEQ // 4)

            def up(p, slot, i, z_bank):
                pe.wait_ge(lo_made, p + 1)
                for k in range(KD):
                    e = slice(k * P, (k + 1) * P)
                    last = three(ps[:, z_bank, :], hi[:, slot, e], lo[:, slot, e], actT_hi[:, k, :], actT_lo[:, k, :],
                                 k == 0, k == KD - 1)
                last.then_inc(ring_free, 1)

            def down(p, slot, g, c, par):
                pe.wait_ge(lo_made, p + 1)
                if c == 0:
                    pe.wait_ge(alo_made, 4 * g + 4)
                for u in range(2):
                    pe.wait_ge(y_added, 16 * g + (4 * c + 2 * u + 2 - 0))
                    for e in range(GROUP):
                        cols = slice(e * BANK, (e + 1) * BANK)
                        for t in range(2):
                            a = slice((2 * u + t) * P, (2 * u + t + 1) * P)
                            last = three(ps[:, 4 + 2 * u + t, :], a_hi[:, par, e, a], a_lo[:, par, e, a],
                                         hi[:, slot, cols], lo[:, slot, cols], e == 0, e == GROUP - 1)
                    last.then_inc(ring_free if u else y_mm, 1)

            pe.sem_inc(y_added, 4)
            for c in range(GROUP):
                if c >= 2:
                    pe.wait_ge(gelu_made, c - 1)
                up(P_PEER + c, c % 2, c, c % 2)

            def group(g, par):
                for c in range(GROUP):
                    p = 8 * g + (2 * c + P_PEER - GROUP)
                    pe.wait_ge(gelu_made, 4 * g + (c - 1))
                    up(p, 0, 4 * g + c, c % 2)
                    down(p + 1, 1, g - 1, c, 1 - par)

            with pe.Fori(0, (N_GROUPS - 2) // 2) as r:
                group(2 * r + 1, 1)
                group(2 * r + 2, 0)
            group(N_GROUPS - 1, 1)
            for c in range(GROUP):
                m = P_PEER + 2 * N_GROUPS * GROUP - GROUP + c
                down(m, m % 2, N_GROUPS - 1, c, 1)


def kernel(x, norm_mix, w_in, q_norm, k_norm, sg_norm, sg_w, sg_b, out_norm_sb, out_norm_sg,
           w_out, norm_ffn, peer_w_query, peer_sub_keys, peer_u, peer_v):
    import numpy as np
    import concourse.bacc as bacc
    from concourse.bass_utils import run_bass_kernel_spmd

    def laid(a, *axes):
        return np.ascontiguousarray(np.transpose(a, axes) if axes else a)

    def pieces(w):
        n = w.shape[1] // BANK
        return laid(np.reshape(w, (KQ, 4, P, n, BANK)), 3, 0, 2, 1, 4).reshape(n * KQ, P, PIECE)

    def by_block(g):
        return laid(np.reshape(g, (-1, P)), 1, 0)

    f = np.asarray
    arrays = {
        "x": laid(f(x)[0]),
        "norm_mix": by_block(f(norm_mix)[0]),
        "norm_ffn": by_block(f(norm_ffn)[0]),
        "norm_y": by_block(np.concatenate([f(out_norm_sb)[0], f(out_norm_sg)[0]])),
        "q_norm": laid(f(q_norm)[0].reshape(P, 1)),
        "k_norm": laid(f(k_norm)[0].reshape(P, 1)),
        "sg_norm": laid(np.broadcast_to(f(sg_norm)[0].reshape(1, WIDTH), (P, WIDTH))),
        "sg_w": laid(f(sg_w)[0], 2, 0, 1),
        "sg_b": laid(f(sg_b)[0], 1, 0),
        "keys": laid(f(peer_sub_keys)[0], 2, 0, 1),
        "w_in": pieces(f(w_in)[0]),
        "w_out": pieces(f(w_out)[0]),
        "w_query": pieces(f(peer_w_query)[0]),
        "peer_u": laid(np.reshape(f(peer_u)[0], (NK, P, KD, P)), 0, 3, 2, 1).reshape(NK, P, PIECE),
        "peer_v": laid(np.reshape(f(peer_v)[0], (N_GROUPS, GROUP, P, 4, BANK)), 0, 3, 2, 1, 4)
        .reshape(NK, P, PIECE),
    }
    nc = bacc.Bacc("TRN2", target_bir_lowering=False, num_devices=1)
    args = [nc.dram_tensor(n, a.shape, mybir.dt.from_np(a.dtype), kind="ExternalInput").ap()
            for n, a in arrays.items()]
    out = nc.dram_tensor("y", (SEQ, D), F32, kind="ExternalOutput").ap()
    layer(nc, *args, out)
    r = run_bass_kernel_spmd(nc, [arrays], core_ids=[0])
    return r.results[0]["y"].reshape(1, SEQ, D)
```

```python
from contextlib import ExitStack

import concourse.bass as bass
from concourse import mybir

ALU = mybir.AluOpType
ACT = mybir.ActivationFunctionType
AX_X = mybir.AxisListType.X
F32 = mybir.dt.float32
F32R = mybir.dt.float32r
U32 = mybir.dt.uint32

P = 128
SEQ = 512
TT = SEQ // P
D = 2048
KD = D // P
HEADS = 8
HD = 128
WIDTH = HEADS * HD
PARTS = 5
Q_PART, K_PART, V_PART, U_PART, G_PART = range(PARTS)
NBANK = 8
BANK = 512
EPS = 1e-6
BIG = 1.0e30

PH = 8
NK = 128
TOPK = 16
NEG = -3.0e38

PIECE = 2048
KQ = 4
IN_CHUNKS = PARTS * WIDTH // BANK
IN_PIECES = IN_CHUNKS * KQ
MM_PIECES = D // BANK * KQ
P_OUT = IN_PIECES
P_QUERY = P_OUT + MM_PIECES
P_PEER = P_QUERY + MM_PIECES
GROUP = 4
N_GROUPS = NK // GROUP
NEAR = SEQ - P
NT = NEAR // P
FAR = TT - 1
PRE = 64
PRE_GROUPS = PRE // GROUP
P_DOWN = P_PEER + PRE
P_BOTH = P_DOWN + GROUP * (PRE_GROUPS - 1)
P_LAST = P_BOTH + 2 * GROUP * (N_GROUPS - PRE_GROUPS)
GSTEP = 64
RING_SLOTS = 2
SCALE = float(HD) ** -0.5
AHEAD_FAR, AHEAD_NEAR, AHEAD_GATES, AHEAD_TAIL = 8, (8, 8, 6), 10, 4
AHEAD_1 = AHEAD_FAR + sum(AHEAD_NEAR)
AHEAD_2 = AHEAD_1 + AHEAD_GATES * (NEAR // GSTEP // 2)
assert AHEAD_2 + AHEAD_TAIL == PRE

IN_NORM, MIX_NORM, FFN_NORM = range(3)

BATCH = 4
GATHER_BUFS = 4


def steps(text):
    return [[(x[0], int(x[1]), int(x[2])) for x in part.split()] for part in text.split("|")]


DOWN_GATHERS = steps("u00 | u01 | u02 | u03 | v00 | v01 | v02 | v03")
DOWN_GELUS = {4: 0}
TAIL_GATHERS = steps("u00 u01 | u02 u03 | v00 v01 | v02 v03")
TAIL_GELUS = {2: 0}
BOTH_GATHERS = steps("u00 u01 u02 | u03 u10 u11 | v00 v01 v02 | v03 u12 u13 | u20 u21 u22 | u23 v10 v11 |"
                     " v12 v13 v20 | v21 v22 v23")
BOTH_GELUS = {2: 0, 4: 1, 6: 2}


def layer(nc, x, nm, nf, ny, qn, kn, sgn, sgw, sgb, keys, w_in, w_out, w_q, pu, u_rows, pv, nf_row, out):
    gates = nc.dram_tensor("gates_scratch", (NK, NK, NEAR), F32).ap()
    spill = nc.dram_tensor("gelu_scratch", (PRE, P, NEAR), F32).ap()

    base = [16512]

    def at(name, shape, dt, kb):
        return nc.alloc_sbuf_tensor_at(name, shape, dt, offset=base[0] + int(kb * 1024))

    actT_hi = at("actT_hi", [P, KD, SEQ], F32R, 0)
    actT_lo = at("actT_lo", [P, KD, SEQ], F32R, 32)
    raw = at("ring_raw", [P, RING_SLOTS, PIECE], F32, 64)
    hi = at("ring_hi", [P, RING_SLOTS, PIECE], F32R, 80)
    lo = at("ring_lo", [P, RING_SLOTS, PIECE], F32R, 96)
    proj = at("proj", [P, PARTS, TT, WIDTH], F32, 112)
    x0 = at("x0", [P, TT, D], F32, 112)
    junk0 = at("junk0", [P, D], F32, 160)
    qk_n = at("qk_n", [P, 2, 2, TT, HD], F32, 0)
    qkT = at("qkT", [P, 2, 2, SEQ], F32, 8)
    v_h = at("v_h", [P, 2, TT, HD], F32, 16)
    sp_t = at("sp_t", [P, 2, 1280], F32, 20)
    sp = at("sp", [P, 2, 1280], F32, 30)
    w_att = at("w_att", [P, 2, 1280], F32, 40)
    x1 = at("x1", [P, TT, D], F32, 128)
    x1n = at("x1n", [P, TT, D], F32, 160)
    junk1 = at("junk1", [P, D], F32, 176)
    junk2 = at("junk2", [P, D], F32, 112)
    sqh = at("sqh", [P, PH, SEQ], F32, 112)
    qT = at("qT", [P, 2 * PH, SEQ], F32, 160)
    s_sb = at("s_sb", [P, 2 * PH, NK], F32, 112)
    eq = at("eq", [P, PH * TOPK, TOPK], F32, 112)
    cand = at("cand", [P, PH, TOPK, TOPK], F32, 120)
    posu = at("posu", [P, 2, PH * TOPK], U32, 120)
    posf = at("posf", [P, 2, PH * TOPK], F32, 121)
    gate_e = at("gate_e", [P, PH, TOPK], F32, 122)
    sel = at("sel", [P, 3, P], F32, 122.5)
    i12f = at("i12f", [P, 2 * PH, TOPK], F32, 124)
    v12 = at("v12", [P, 2 * PH, TOPK], F32, 196)
    i12u = at("i12u", [P, 2 * PH, TOPK], U32, 197)
    tv = at("tv", [P, PH, TOPK], F32, 198)
    tpos = at("tpos", [P, PH, TOPK], U32, 198.5)
    gate_s = at("gate_s", [P, 2, PH], F32, 199)
    gbuf = at("gbuf", [P, NK, GSTEP], F32, 160)
    hot_a = at("hot_a", [P, 16, NK], F32, 112)
    hot_b = at("hot_b", [P, 16, NK], F32, 120)
    free_hi = at("free_hi", [P, KD, SEQ], F32, 0)[:, :, NEAR:SEQ]
    free_lo = at("free_lo", [P, KD, SEQ], F32, 32)[:, :, NEAR:SEQ]
    ahead = [free_hi[:, 3 * b:3 * b + 3, :] for b in range(2)]
    h_far = free_hi
    gch = [free_lo[:, 3 * c:3 * c + 3, :] for c in range(GROUP)]
    gelu = at("gelu", [P, 2, NEAR], F32, 124)
    g_in = [free_lo[:, 12:15, :], at("g_in_1", [P, NT, P], F32, 190)[:]]
    a_hi = at("a_hi", [P, 2, GROUP, NEAR], F32R, 112)
    a_lo = [at("a_lo_0", [P, GROUP, NEAR], F32R, 200), at("a_lo_1", [P, GROUP, NEAR], F32R, 184)]
    rows = [at(f"rows_{b}", [P, D], F32, kb) for b, kb in enumerate((160, 168, 176, 192))]
    ident = at("ident", [P, P], F32, 192)
    tri = at("tri", [P, P], F32, 192.5)
    neg1 = at("neg1", [P, P], F32, 193)
    keep = at("keep", [P, P], F32, 193.5)
    block_m = at("block_m", [P, P], F32, 194)
    iota = at("iota128", [P, NK], F32, 194.5)
    keysT = at("keysT", [P, 2, NK], F32, 195)
    sq = at("sq", [P, 2, BANK], F32, 196)
    selT = at("selT", [P, 3, NEAR], F32, 200)
    iota16 = at("iota16", [P, TOPK], F32, 206)
    small = at("small", [P, 110], F32, 206.0625)
    stats = at("stats", [P, PARTS, TT, HEADS], F32, 206.5)
    gains = small[:, 0:48].rearrange("p (s k) -> p s k", s=3)
    qgain, kgain, sgb_s = small[:, 48:49], small[:, 49:50], small[:, 50:58]
    ss = small[:, 58:66]
    rq = small[:, 66:98].rearrange("p (t h) -> p t h", t=TT)
    tick, pool_ticks = small[:, 98:99], small[:, 99:101]
    idx_far = at("idx_far", [P, P], U32, 206.5)
    z_far = at("z_far", [P, 3 * BATCH], F32, 207)
    a_far = at("a_far", [P, 3 * BATCH], F32, 207.0625)
    idx_now = at("idx_now", [P, GATHER_BUFS], U32, 207.125)
    gate_far = at("gate_far", [P, P], F32, 207.25)
    sgw_s = at("sgw_s", [P, HEADS, P], F32, 52)
    sgn_s = at("sgn_s", [P, WIDTH], F32, 56)

    with ExitStack() as ctx:
        ps = ctx.enter_context(nc.psum_tensor("ps", [P, NBANK, BANK], F32))

        def sem(name):
            return ctx.enter_context(nc.semaphore(name))

        s_par = sem("params_loaded")
        s_x = [sem(f"x_loaded_{t}") for t in range(TT)]
        s_const = sem("constants_made")
        raw_full = [sem(f"raw_full_{s}") for s in range(RING_SLOTS)]
        hi_made = sem("hi_made")
        lo_made = sem("lo_made")
        ring_free = sem("ring_free")
        row_sq = [sem(f"row_squares_{s}") for s in range(3)]
        var_made = [sem(f"variance_{s}") for s in range(3)]
        rooted = [sem(f"rooted_{s}") for s in range(3)]
        inverted = [sem(f"inverted_{s}") for s in range(3)]
        normed = [sem(f"rows_normed_{s}") for s in range(3)]
        turned = [sem(f"turned_{s}") for s in range(3)]
        t_hi = [sem(f"turned_hi_{s}") for s in range(3)]
        t_lo = [sem(f"turned_lo_{s}") for s in range(3)]
        proj_out = sem("proj_copied_out")
        squared = sem("proj_squared")
        reduced = sem("proj_squares_reduced")
        st_var, st_root, st_inv = sem("stats_var"), sem("stats_rooted"), sem("stats_inverted")
        s_sgp = sem("gmlp_params_loaded")
        s_sgm = sem("gmlp_masked")
        vb_made, mixed, gated = sem("vb_made"), sem("mixed"), sem("gated")
        qk_normed, v_copied = sem("qk_normed"), sem("v_copied")
        qk_turned, qkT_out = sem("qk_turned"), sem("qkT_out")
        z_done, z_abs, z_exp, z_ln = sem("z_done"), sem("z_abs"), sem("z_exp"), sem("z_ln")
        sp_made, sp_kept = sem("sp_made"), sem("sp_kept")
        tails, z_blocked, w_made = sem("tails"), sem("z_blocked"), sem("w_made")
        pv_done, y_out = sem("pv_done"), sem("y_out")
        s_x1 = sem("x1_loaded")
        out_added = sem("out_added")
        q_out, q_sq, q_pair = sem("q_out"), sem("q_squared"), sem("q_pair_added")
        q_ss, q_var, q_root, q_inv = sem("q_ss"), sem("q_var"), sem("q_root"), sem("q_inv")
        s_done, s_out, topk, sm_sub, sm_exp = (sem("scores_done"), sem("scores_out"), sem("topk_step"),
                                               sem("softmax_sub"), sem("softmax_exp"))
        sel_made, sel_turned, selT_out = sem("sel_made"), sem("sel_turned"), sem("selT_out")
        hot_made, g_mm, g_out, g_stored = sem("hot_made"), sem("g_mm"), sem("g_out"), sem("g_stored")
        ahead_stored = [sem(f"ahead_stored_{b}") for b in range(2)]
        g_loaded = [sem(f"gate_loaded_{c}") for c in range(GROUP)]
        gin_loaded = [sem(f"gelu_loaded_{b}") for b in range(2)]
        gelu_made, act_made, ahi_made, alo_made = (sem("gelu_made"), sem("act_made"), sem("a_hi_made"),
                                                   sem("a_lo_made"))
        y_added = sem("expert_y_added")
        far_sel, nf_loaded, h_far_made = sem("far_selected"), sem("norm_row_loaded"), sem("h_far_made")
        idx_copied = sem("idx_copied")
        gathered = [sem(f"gathered_{b}") for b in range(GATHER_BUFS)]
        row_used = sem("row_used")
        far_gelu, far_weight = sem("far_gelu"), sem("far_weight")
        s_stored = sem("out_stored")

        block = ctx.enter_context(nc.Block())

        def turned_from(stage, tt, k):
            if stage == IN_NORM:
                return x0[:, tt, k * P:(k + 1) * P]
            if stage == FFN_NORM:
                return x1n[:, tt, k * P:(k + 1) * P]
            part, k = (Q_PART, k) if k < HEADS else (U_PART, k - HEADS)
            return proj[:, part, tt, k * P:(k + 1) * P]

        def bcast(ap, shape, *axes):
            for a in axes:
                ap = ap.unsqueeze(a)
            return ap.broadcast_to(shape)

        @block.sync
        def _(sp_eng):
            for t in range(TT):
                sp_eng.dma_start(x0[:, t, :], x[t * P:(t + 1) * P, :]).then_inc(s_x[t], 16)

            def load(src, p, slot, n):
                sp_eng.wait_ge(lo_made, p - 1)
                sp_eng.dma_start(raw[:, slot, :], src[bass.ds(n, 1)].rearrange("a p n -> p (a n)"))\
                      .then_inc(raw_full[slot], 16)

            for p in range(RING_SLOTS):
                sp_eng.dma_start(raw[:, p, :], w_in[p]).then_inc(raw_full[p], 16)
            with sp_eng.Fori(1, IN_PIECES // 2) as i:
                for s in range(2):
                    load(w_in, 2 * i + s, s, 2 * i + s)
            for src, first in ((w_out, P_OUT), (w_q, P_QUERY)):
                with sp_eng.Fori(0, MM_PIECES // 2) as i:
                    for s in range(2):
                        load(src, 2 * i + s + first, s, 2 * i + s)
            with sp_eng.Fori(0, PRE // 2) as i:
                for s in range(2):
                    load(pu, 2 * i + s + P_PEER, s, 2 * i + s)

            def load_v(p, slot, g, c):
                sp_eng.wait_ge(lo_made, p - 1)
                src = pv.rearrange("(g el e) d -> g e el d", el=GROUP, e=P)[bass.ds(g, 1), :, :,
                                                                            c * BANK:(c + 1) * BANK]
                sp_eng.dma_start(raw[:, slot, :].rearrange("p (el d) -> p el d", el=GROUP),
                                 src.rearrange("g e el d -> e (g el) d")).then_inc(raw_full[slot], 16)

            def load_gate(i, c):
                sp_eng.dma_start(gch[c], gates[bass.ds(i, 1)].rearrange("a j (b t) -> j (a b) t", t=P))\
                      .then_inc(g_loaded[c], 16)

            def load_gelu(i, b):
                sp_eng.dma_start(g_in[b], spill[bass.ds(i, 1)].rearrange("a e (b t) -> e (a b) t", t=P))\
                      .then_inc(gin_loaded[b], 16)

            load_v(P_DOWN, 0, 0, 0)
            sp_eng.wait_ge(g_stored, 16 * (NEAR // GSTEP) + 16)
            for b in range(2):
                sp_eng.wait_ge(ahead_stored[b], 16 * (GROUP // 2) + 16)
            for c in range(GROUP):
                load_gate(c, c)
                if c >= 2:
                    sp_eng.wait_ge(alo_made, c - 1)
                load_gelu(c, c % 2)
            for b in range(2):
                sp_eng.wait_ge(ahead_stored[b], 16 * (PRE // 2) + 16)

            def down_group(g, last):
                for c in range(GROUP):
                    i = GROUP * g + c
                    if c < GROUP - 1:
                        load_v(4 * g + (c + P_DOWN - GROUP + 1), (c + 1) % 2, g - 1, c + 1)
                    elif not last:
                        load_v(4 * g + P_DOWN, 0, g, 0)
                    sp_eng.wait_ge(act_made, i - 3)
                    load_gate(i, c)
                    sp_eng.wait_ge(alo_made, i - 1)
                    load_gelu(i, c % 2)

            with sp_eng.Fori(1, PRE_GROUPS - 1) as g:
                down_group(g, False)
            with sp_eng.Fori(PRE_GROUPS - 1, PRE_GROUPS) as g:
                down_group(g, True)
            with sp_eng.Fori(PRE_GROUPS, N_GROUPS) as g:
                for c in range(GROUP):
                    p = 8 * g + (P_BOTH - 8 * PRE_GROUPS + 2 * c)
                    sp_eng.wait_ge(act_made, GROUP * g + (c - 3))
                    load_gate(GROUP * g + c, c)
                    load(pu, p, 0, GROUP * g + c)
                    load_v(p + 1, 1, g - 1, c)
            for c in range(GROUP):
                load_v(P_LAST + c, c % 2, N_GROUPS - 1, c)
            sp_eng.wait_ge(y_added, NT * GROUP * N_GROUPS + 6)
            sp_eng.wait_ge(row_used, 2 * P + GATHER_BUFS)
            for t in range(TT):
                sp_eng.dma_start(out[t * P:(t + 1) * P, :], x1[:, t, :]).then_inc(s_stored, 16)
            sp_eng.wait_ge(s_stored, 16 * TT)

        @block.gpsimd
        def _(pool):
            made = [0]

            def const(ins):
                made[0] += 1
                ins.then_inc(s_const, 1)
                pool.wait_ge(s_const, made[0])

            for dst, src in ((gains[:, 0, :], nm), (gains[:, 1, :], ny), (gains[:, 2, :], nf), (qgain, qn),
                             (kgain, kn), (sgb_s, sgb), (keysT[:], keys)):
                pool.dma_start(dst, src).then_inc(s_par, 16)
            const(pool.memset(ident[:], 0.0))
            const(pool.affine_select(out=ident[:], in_=ident[:], compare_op=ALU.not_equal, fill=1.0, base=0,
                                     pattern=[[-1, P]], channel_multiplier=1))
            const(pool.memset(neg1[:], -1.0))
            const(pool.affine_select(out=tri[:], in_=neg1[:], compare_op=ALU.is_ge, fill=0.0, base=0,
                                     pattern=[[-1, P]], channel_multiplier=1))
            const(pool.memset(keep[:], 1.0))
            const(pool.affine_select(out=keep[:], in_=keep[:], compare_op=ALU.is_gt, fill=0.0, base=0,
                                     pattern=[[1, P]], channel_multiplier=-1))
            const(pool.memset(block_m[:], 0.0))
            const(pool.affine_select(out=block_m[:], in_=block_m[:], compare_op=ALU.is_gt, fill=-BIG, base=0,
                                     pattern=[[1, P]], channel_multiplier=-1))
            const(pool.iota(iota[:], [[1, NK]], base=0, channel_multiplier=0,
                            allow_small_or_imprecise_dtypes=True))
            const(pool.iota(iota16[:], [[1, TOPK]], base=0, channel_multiplier=0,
                            allow_small_or_imprecise_dtypes=True))
            pool.wait_ge(ring_free, RING_SLOTS + IN_PIECES)
            pool.dma_start(sgw_s[:], sgw).then_inc(s_sgp, 16)
            pool.dma_start(sgn_s[:], sgn).then_inc(s_sgp, 16)
            for i in range(HEADS // 2):
                if i:
                    pool.wait_ge(pv_done, 2 * i)
                for ab in range(2):
                    pool.wait_ge(proj_out, 4 * IN_CHUNKS)
                    pool.tensor_copy(v_h[:, ab, :, :], proj[:, V_PART, :, bass.ds((2 * i + ab) * HD, HD)])\
                        .then_inc(v_copied, 1)
            pool.wait_ge(pv_done, HEADS)
            pool.wait_ge(v_copied, HEADS)
            pool.dma_start(x1[:], x.rearrange("(t p) d -> p t d", p=P)).then_inc(s_x1, 16)

            pool.wait_ge(lo_made, P_PEER)

            def make_lo(p, slot):
                pool.wait_ge(hi_made, p + 1)
                pool.tensor_tensor(lo[:, slot, :], raw[:, slot, :], hi[:, slot, :].bitcast(F32), ALU.subtract)\
                    .then_inc(lo_made, 1)

            with pool.Fori(0, PRE // 2) as i:
                for s in range(2):
                    make_lo(2 * i + (P_PEER + s), s)
            make_lo(P_DOWN, 0)

            pool.wait_ge(g_stored, 16 * (NEAR // GSTEP) + 16)
            pool.dma_start(rows[0][:], nf_row).then_inc(nf_loaded, 16)
            pool.wait_ge(far_sel, 2)
            pool.wait_ge(h_far_made, 1)

            def carry(k):
                pool.tensor_tensor(pool_ticks[:, k:k + 1], kgain, kgain, ALU.add)

            def gather(parts, q, b):
                n = 0
                for part in parts:
                    for kind, batch, slot in part:
                        buf = n % GATHER_BUFS
                        pool.wait_ge(row_used, q + (n + 1))
                        carry(0)
                        pool.tensor_copy(idx_now[:, buf:buf + 1],
                                         idx_far[:, bass.ds(BATCH * b + (BATCH * batch + slot), 1)])\
                            .then_inc(idx_copied, 1)
                        pool.wait_ge(idx_copied, q + (n + 1))
                        carry(1)
                        pool.indirect_dma_start(
                            out=rows[buf][:], out_offset=None, in_=u_rows if kind == "u" else pv,
                            in_offset=bass.IndirectOffsetOnAxis(ap=idx_now[:, buf:buf + 1], axis=0))\
                            .then_inc(gathered[buf], 16)
                        n += 1

            with pool.Fori(0, PRE_GROUPS // 2 - 1) as r:
                gather(DOWN_GATHERS, 8 * r, r)
            with pool.Fori(0, 1) as r:
                gather(TAIL_GATHERS, 8 * r + 4 * PRE_GROUPS - 8, r + PRE_GROUPS // 2 - 1)
            with pool.Fori(0, (N_GROUPS - PRE_GROUPS) // 2) as r:
                gather(BOTH_GATHERS, 24 * r + 4 * PRE_GROUPS, 3 * r + PRE_GROUPS // 2)

        @block.scalar
        def _(act):
            def make_hi(p, slot, use):
                act.wait_ge(raw_full[slot], 16 * use)
                act.wait_ge(ring_free, p + 1)
                act.activation(hi[:, slot, :], raw[:, slot, :], ACT.Copy).then_inc(hi_made, 1)

            def root(stage, cols):
                act.wait_ge(var_made[stage], 1)
                act.activation(ss[:, 0:cols], ss[:, 0:cols], ACT.Sqrt).then_inc(rooted[stage], 1)

            def turn_hi(stage):
                for k in range(KD):
                    act.wait_ge(turned[stage], k + 1)
                    act.activation(actT_hi[:, k, :], ps[:, k % NBANK, :], ACT.Copy,
                                   scale=gains[:, stage, k:k + 1]).then_inc(t_hi[stage], 1)

            for t in range(TT):
                act.wait_ge(s_x[t], 16)
                act.activation(junk0[:], x0[:, t, :], ACT.Square, accum_out=ss[:, t:t + 1])\
                   .then_inc(row_sq[IN_NORM], 1)
                act.wait_ge(row_sq[IN_NORM], t + 1)
            root(IN_NORM, TT)
            act.wait_ge(s_par, 16 * 7)
            turn_hi(IN_NORM)

            def evac_in(c, i, part, cc, func):
                act.wait_ge(ring_free, 4 * c + (4 + RING_SLOTS))
                for t in range(TT):
                    dst = proj[:, bass.ds(part, 1), t, cc * BANK:(cc + 1) * BANK].rearrange("p a n -> p (a n)")
                    act.activation(dst, ps[:, cc * 4 + t, :], func).then_inc(proj_out, 1)
                    act.wait_ge(proj_out, 4 * c + t + 1)
                    act.wait_ge(reduced, 4 * c + t + 1)
                    act.activation(sq[:, t % 2, :], dst, ACT.Square).then_inc(squared, 1)

            act.sem_inc(reduced, 2)
            act.wait_ge(raw_full[0], 16)
            make_hi(0, 0, 1)
            for first, count, func in ((0, 3, ACT.Copy), (3, 2, ACT.Gelu)):
                for i in range(first, first + count):
                    for cc in range(2):
                        for kq in range(KQ):
                            n = 4 * cc + kq + 1
                            make_hi(8 * i + n, n % 2, 4 * i + n // 2 + 1)
                        evac_in(2 * i + cc, i, i, cc, func)
            act.wait_ge(st_var, 1)
            st = stats[:].rearrange("p a t h -> p (a t h)")
            act.activation(st, st, ACT.Sqrt).then_inc(st_root, 1)

            for i in range(HEADS // 2):
                for ab in range(2):
                    n = 2 * i + ab
                    for j, gain in ((0, qgain), (1, kgain)):
                        act.wait_ge(qk_turned, 2 * n + j + 1)
                        act.activation(qkT[:, ab, j, :], ps[:, 7 * j, :], ACT.Copy, scale=gain)\
                           .then_inc(qkT_out, 1)
                for ab in range(2):
                    n = 2 * i + ab
                    z = ps[:, 1 + 3 * ab:4 + 3 * ab, :].rearrange("p b n -> p (b n)")[:, 0:1280]
                    act.wait_ge(z_done, n + 1)
                    act.activation(sp_t[:, ab, :], z, ACT.Abs).then_inc(z_abs, 1)
                    act.wait_ge(z_abs, n + 1)
                    act.activation(sp_t[:, ab, :], sp_t[:, ab, :], ACT.Exp, scale=-1.0).then_inc(z_exp, 1)
                    act.wait_ge(z_exp, n + 1)
                    act.activation(sp_t[:, ab, :], sp_t[:, ab, :], ACT.Ln, bias=1.0).then_inc(z_ln, 1)
                for ab in range(2):
                    n = 2 * i + ab
                    z = ps[:, 1 + 3 * ab:4 + 3 * ab, :].rearrange("p b n -> p (b n)")[:, 0:1280]
                    act.wait_ge(z_blocked, 2 * n + 2)
                    act.activation(w_att[:, ab, :], z, ACT.Exp).then_inc(w_made, 1)
                for ab in range(2):
                    n = 2 * i + ab
                    act.wait_ge(pv_done, n + 1)
                    act.activation(proj[:, Q_PART, :, bass.ds(n * HD, HD)],
                                   ps[:, 7 * ab, :].rearrange("p (t c) -> p t c", t=TT), ACT.Copy)\
                       .then_inc(y_out, 1)

            act.wait_ge(y_out, HEADS + 1)
            act.wait_ge(gated, HEADS)
            n = 0
            for j, part in enumerate((Q_PART, U_PART)):
                for t in range(TT):
                    act.activation(junk1[:, 0:WIDTH], proj[:, part, t, :], ACT.Square,
                                   accum_out=ss[:, j * TT + t:j * TT + t + 1]).then_inc(row_sq[MIX_NORM], 1)
                    n += 1
                    act.wait_ge(row_sq[MIX_NORM], n)
            root(MIX_NORM, 2 * TT)
            turn_hi(MIX_NORM)
            with act.Fori(0, MM_PIECES // 2) as i:
                for s in range(2):
                    make_hi(2 * i + (P_OUT + 1 + s), (1 + s) % 2, i + (P_OUT // 2 + 1 + s))
            for t in range(TT):
                act.wait_ge(out_added, 8 + 16)
                act.activation(junk2[:], x1[:, t, :], ACT.Square, accum_out=ss[:, t:t + 1])\
                   .then_inc(row_sq[FFN_NORM], 1)
                act.wait_ge(row_sq[FFN_NORM], t + 1)
            root(FFN_NORM, TT)
            turn_hi(FFN_NORM)

            for c in range(4):
                for kq in range(KQ):
                    m = 4 * c + kq + 1
                    if m < MM_PIECES:
                        make_hi(P_QUERY + m, m % 2, (P_QUERY + m) // 2 + 1)
                act.wait_ge(ring_free, P_QUERY + 4 * c + 4 + RING_SLOTS)
                for b in range(4):
                    m = 4 * c + b
                    act.activation(qT[:, m, :], ps[:, (c % 2) * 4 + b, :], ACT.Copy).then_inc(q_out, 1)
                    if m >= 2:
                        act.wait_ge(q_pair, m // 2)
                    act.activation(sq[:, b % 2, :], ps[:, (c % 2) * 4 + b, :], ACT.Square).then_inc(q_sq, 1)
            act.wait_ge(q_var, 1)
            act.activation(rq, rq, ACT.Sqrt).then_inc(q_root, 1)

            def ahead_tile(half, b, last=False):
                i, p = 2 * half + b, 2 * half + (b + P_PEER)
                act.wait_ge(ring_free, p + (1 + RING_SLOTS))
                act.wait_ge(ahead_stored[b], 16 * half + 16)
                act.activation(ahead[b], ps[:, b, 0:NEAR].rearrange("p (b t) -> p b t", t=P), ACT.Gelu)\
                   .then_inc(gelu_made, 1)
                if not last:
                    make_hi(p + 2, b, half + (P_PEER // 2 + 2))
                act.wait_ge(gelu_made, i + 3)
                act.dma_start(spill[bass.ds(i, 1)].rearrange("a e (b t) -> e (a b) t", t=P), ahead[b])\
                   .then_inc(ahead_stored[b], 16)

            for s in range(2):
                make_hi(P_PEER + s, s, P_PEER // 2 + 1)
            for b in range(2):
                act.sem_inc(ahead_stored[b], 16)

            def softmax_exp(m):
                act.wait_ge(sm_sub, m + 1)
                act.activation(gate_e[:], gate_e[:], ACT.Exp).then_inc(sm_exp, 1)

            first = 0
            for m, count in enumerate((AHEAD_FAR,) + AHEAD_NEAR):
                exp_at = first // 2 + (count // 2 - 1)
                with act.Fori(first // 2, exp_at) as h:
                    for b in range(2):
                        ahead_tile(h, b)
                softmax_exp(m)
                with act.Fori(exp_at, exp_at + 1) as h:
                    for b in range(2):
                        ahead_tile(h, b)
                first += count

            act.sem_inc(g_stored, 16)
            waited = act.alloc_register("waited")

            def copy_gates(b, quad):
                for j in range(4 * quad, 4 * quad + 4):
                    act.wait_ge(g_mm, 16 * b + (j + 1 + 4))
                    act.reg_mov(waited, 0)
                    act.activation(gbuf[:, :, 4 * j:4 * j + 4],
                                   ps[:, 2 + j % 4, :].rearrange("p (t i) -> p i t", t=4), ACT.Copy)\
                       .then_inc(g_out, 1)

            with act.Fori(0, NEAR // GSTEP // 2) as r:
                for s in range(2):
                    b = 2 * r + s

                    def ahead_of(n):
                        at = AHEAD_1 + AHEAD_GATES // 2 * s + n
                        ahead_tile(AHEAD_GATES // 2 * r + at // 2, at % 2)

                    ahead_of(0)
                    ahead_of(1)
                    act.wait_ge(g_stored, 16 * b + 16)
                    act.reg_mov(waited, 0)
                    copy_gates(b, 0)
                    for quad in range(1, 4):
                        ahead_of(quad + 1)
                        copy_gates(b, quad)
                    act.wait_ge(g_out, 16 * b + (16 + 4))
                    act.dma_start(gates.rearrange("i j t -> j i t")[:, :, bass.ds(GSTEP * b, GSTEP)], gbuf[:])\
                       .then_inc(g_stored, 16)
            with act.Fori(AHEAD_2 // 2, PRE // 2 - 1) as h:
                for b in range(2):
                    ahead_tile(h, b)
            with act.Fori(PRE // 2 - 1, PRE // 2) as h:
                for b in range(2):
                    ahead_tile(h, b, last=b == 1)

            def a_hi_of(i, par, c, src):
                act.wait_ge(act_made, i + 1)
                act.activation(a_hi[:, par, c, :].rearrange("p (b t) -> p b t", t=P), src, ACT.Copy)\
                   .then_inc(ahi_made, 1)

            def gelu_far(gelus, parts, part, q, b):
                if part in gelus:
                    batch = gelus[part]
                    flat = [x for one in parts for x in one]
                    n = flat.index(("u", batch, BATCH - 1)) + 1
                    cols = slice(BATCH * batch, BATCH * (batch + 1))
                    act.wait_ge(row_used, q + (n + GATHER_BUFS))
                    act.activation(a_far[:, cols], z_far[:, cols], ACT.Gelu).then_inc(far_gelu, 1)

            def down_group(g, par, part, gelus, parts, q, b):
                for c in range(GROUP):
                    gelu_far(gelus, parts, part + c, q, b)
                    make_hi(4 * g + (c + P_DOWN - GROUP + 1), (c + 1) % 2,
                            2 * g + ((P_DOWN - GROUP) // 2 + (c + 1) // 2 + 1))
                    a_hi_of(4 * g + c, par, c, g_in[c % 2])

            def both_group(g, par, part, q, b):
                for c in range(GROUP):
                    p = 8 * g + (2 * c + P_BOTH - 8 * PRE_GROUPS)
                    use = 4 * g + (c + (P_BOTH - 8 * PRE_GROUPS) // 2 + 1)
                    gelu_far(BOTH_GELUS, BOTH_GATHERS, part + c, q, b)
                    make_hi(p + 1, 1, use)
                    make_hi(p + 2, 0, use + 1)
                    act.wait_ge(ring_free, p + (1 + RING_SLOTS))
                    act.wait_ge(alo_made, 4 * g + (c - 1))
                    act.activation(gelu[:, c % 2, :], ps[:, c % 2, 0:NEAR], ACT.Gelu).then_inc(gelu_made, 1)
                    a_hi_of(4 * g + c, par, c, gelu[:, c % 2, :].rearrange("p (b t) -> p b t", t=P))

            for c in range(GROUP):
                a_hi_of(c, 0, c, g_in[c % 2])
            with act.Fori(0, PRE_GROUPS // 2 - 1) as r:
                down_group(2 * r + 1, 1, 0, DOWN_GELUS, DOWN_GATHERS, 8 * r, r)
                down_group(2 * r + 2, 0, 4, DOWN_GELUS, DOWN_GATHERS, 8 * r, r)
            down_group(PRE_GROUPS - 1, 1, 0, TAIL_GELUS, TAIL_GATHERS, 4 * PRE_GROUPS - 8, 0)
            with act.Fori(0, (N_GROUPS - PRE_GROUPS) // 2) as r:
                both_group(2 * r + PRE_GROUPS, 0, 0, 24 * r + 4 * PRE_GROUPS, r)
                both_group(2 * r + (PRE_GROUPS + 1), 1, 4, 24 * r + 4 * PRE_GROUPS, r)
            for c in range(1, GROUP):
                make_hi(P_LAST + c, c % 2, (P_LAST + c) // 2 + 1)

        @block.vector
        def _(dve):
            def make_lo(p, slot):
                dve.wait_ge(hi_made, p + 1)
                dve.tensor_tensor(lo[:, slot, :], raw[:, slot, :], hi[:, slot, :].bitcast(F32), ALU.subtract)\
                   .then_inc(lo_made, 1)

            def inverse_rms(stage, cols, width, n_sq):
                dve.wait_ge(row_sq[stage], n_sq)
                dve.tensor_scalar(ss[:, 0:cols], ss[:, 0:cols], 1.0 / width, EPS, ALU.mult, ALU.add)\
                   .then_inc(var_made[stage], 1)
                dve.wait_ge(rooted[stage], 1)
                dve.reciprocal(ss[:, 0:cols], ss[:, 0:cols]).then_inc(inverted[stage], 1)
                dve.wait_ge(inverted[stage], 1)

            def turn_lo(stage):
                for k in range(KD):
                    dve.wait_ge(t_hi[stage], k + 1)
                    dve.scalar_tensor_tensor(out=actT_lo[:, k, :], in0=ps[:, k % NBANK, :],
                                             scalar=gains[:, stage, k:k + 1], in1=actT_hi[:, k, :].bitcast(F32),
                                             op0=ALU.mult, op1=ALU.subtract).then_inc(t_lo[stage], 1)

            inverse_rms(IN_NORM, TT, D, TT)
            for t in range(TT):
                dve.tensor_scalar(x0[:, t, :], x0[:, t, :], ss[:, t:t + 1], None, ALU.mult)\
                   .then_inc(normed[IN_NORM], 1)
            dve.wait_ge(s_par, 16 * 7)
            turn_lo(IN_NORM)

            def sum_squares(c, part, cc):
                for t in range(TT):
                    dve.wait_ge(squared, 4 * c + (t + 1 + 8))
                    dve.tensor_reduce(stats[:, bass.ds(part, 1), t, 4 * cc:4 * cc + 4].rearrange("p a h -> p (a h)"),
                                      sq[:, t % 2, :].rearrange("p (h c) -> p h c", c=HD), AX_X, ALU.add)\
                       .then_inc(reduced, 1)

            make_lo(0, 0)
            with dve.Fori(0, PARTS) as i:
                for cc in range(2):
                    for kq in range(KQ):
                        n = 4 * cc + kq + 1
                        make_lo(8 * i + n, n % 2)
                    sum_squares(2 * i + cc, i, cc)
            st = stats[:].rearrange("p a t h -> p (a t h)")
            dve.wait_ge(reduced, 4 * IN_CHUNKS + 2)
            dve.tensor_scalar(st, st, 1.0 / HD, EPS, ALU.mult, ALU.add).then_inc(st_var, 1)
            dve.tensor_scalar(qgain, qgain, SCALE, None, ALU.mult).then_inc(st_inv, 1)
            dve.wait_ge(st_root, 1)
            dve.reciprocal(st, st).then_inc(st_inv, 1)
            dve.wait_ge(st_inv, 2)

            dve.wait_ge(s_sgp, 32)
            dve.memset(sgw_s[64:128, :, 0:64], 0.0).then_inc(s_sgm, 1)
            for h in range(HEADS):
                cols = slice(h * HD, (h + 1) * HD)
                for t in range(TT):
                    dve.scalar_tensor_tensor(out=proj[:, G_PART, t, cols], in0=proj[:, G_PART, t, cols],
                                             scalar=stats[:, G_PART, t, h:h + 1], in1=sgn_s[:, cols],
                                             op0=ALU.mult, op1=ALU.mult).then_inc(vb_made, 1)
            for h in range(HEADS):
                cols = slice(h * HD, (h + 1) * HD)
                dve.wait_ge(mixed, h + 1)
                dve.scalar_tensor_tensor(out=proj[:, U_PART, :, cols],
                                         in0=ps[:, h, :].rearrange("p (t c) -> p t c", t=TT),
                                         scalar=sgb_s[:, h:h + 1], in1=proj[:, U_PART, :, cols],
                                         op0=ALU.add, op1=ALU.mult).then_inc(gated, 1)

            with dve.Fori(0, HEADS // 2) as i:
                for ab in range(2):
                    n = 2 * i + ab
                    for j in range(2):
                        r = stats[:, j, :, bass.ds(n, 1)]
                        dve.tensor_tensor(qk_n[:, ab, j, :, :], proj[:, j, :, bass.ds(n * HD, HD)],
                                          r.broadcast_to([P, TT, HD]), ALU.mult).then_inc(qk_normed, 1)
                for ab in range(2):
                    n = 2 * i + ab
                    z = ps[:, 1 + 3 * ab:4 + 3 * ab, :].rearrange("p b n -> p (b n)")
                    dve.wait_ge(z_ln, n + 1)
                    dve.scalar_tensor_tensor(out=sp[:, ab, :], in0=z[:, 0:1280], scalar=0.0, in1=sp_t[:, ab, :],
                                             op0=ALU.max, op1=ALU.add).then_inc(sp_made, 1)
                    dve.wait_ge(sp_made, n + 1)
                    three = sp[:, ab, 0:1280].rearrange("p (b n) -> p b n", n=256)[:, 0:5:2, 0:P]
                    dve.tensor_tensor(three, three, bcast(keep[:], [P, 3, P], 1), ALU.mult).then_inc(sp_kept, 1)
                    dve.tensor_tensor(sp[:, ab, 896:1024], sp[:, ab, 896:1024], keep[:], ALU.mult)\
                       .then_inc(sp_kept, 1)
                for ab in range(2):
                    n = 2 * i + ab
                    z = ps[:, 1 + 3 * ab:4 + 3 * ab, :]
                    dve.wait_ge(tails, n + 1)
                    dve.tensor_tensor(z[:, :, 0:P], z[:, :, 0:P], bcast(block_m[:], [P, 3, P], 1), ALU.add)\
                       .then_inc(z_blocked, 1)
                    dve.tensor_tensor(z[:, 1, 384:512], z[:, 1, 384:512], block_m[:], ALU.add)\
                       .then_inc(z_blocked, 1)

            inverse_rms(MIX_NORM, 2 * TT, WIDTH, 2 * TT)
            for j, part in enumerate((Q_PART, U_PART)):
                for t in range(TT):
                    dve.tensor_scalar(proj[:, part, t, :], proj[:, part, t, :], ss[:, j * TT + t:j * TT + t + 1],
                                      None, ALU.mult).then_inc(normed[MIX_NORM], 1)
            turn_lo(MIX_NORM)
            dve.wait_ge(s_x1, 16)
            with dve.Fori(0, 2) as i:
                for cc in range(2):
                    for kq in range(KQ):
                        n = 4 * cc + kq + 1
                        make_lo(8 * i + (P_OUT + n), n % 2)
                    dve.wait_ge(ring_free, 8 * i + (P_OUT + 4 * cc + 4 + RING_SLOTS))
                    for t in range(TT):
                        col = x1[:, t, bass.ds(i * 2 * BANK + cc * BANK, BANK)]
                        dve.tensor_tensor(col, ps[:, cc * 4 + t, :], col, ALU.add).then_inc(out_added, 1)
            inverse_rms(FFN_NORM, TT, D, TT)
            for t in range(TT):
                dve.tensor_scalar(x1n[:, t, :], x1[:, t, :], ss[:, t:t + 1], None, ALU.mult)\
                   .then_inc(normed[FFN_NORM], 1)
            turn_lo(FFN_NORM)

            for c in range(4):
                for kq in range(KQ):
                    m = 4 * c + kq + 1
                    if m < MM_PIECES:
                        make_lo(P_QUERY + m, m % 2)
                for h in range(2 * c, 2 * c + 2):
                    dve.wait_ge(q_sq, 2 * h + 2)
                    dve.tensor_tensor(sqh[:, h, :], sq[:, 0, :], sq[:, 1, :], ALU.add).then_inc(q_pair, 1)
            dve.wait_ge(q_ss, 1)
            dve.tensor_scalar(rq, ps[:, 0, 0:TT * PH].rearrange("p (t h) -> p t h", t=TT), -1.0 / (2 * HD), EPS,
                              ALU.mult, ALU.add).then_inc(q_var, 1)
            dve.wait_ge(q_root, 1)
            dve.reciprocal(rq, rq).then_inc(q_inv, 1)
            dve.wait_ge(q_inv, 1)

            STEPS = 22

            def retrieve(m, t, far):
                step = [0]

                def done(ins):
                    step[0] += 1
                    ins.then_inc(topk, 1)
                    dve.wait_ge(topk, STEPS * m + step[0])

                def carry():
                    dve.memset(tick, 0.0)

                def top16(count, values, best, places):
                    for half in range(2):
                        eight = slice(8 * half, 8 * half + 8)
                        for what in (0, 1, 2) if not half else (0, 1):
                            carry()
                            for n in range(count):
                                if what == 0:
                                    last = dve.max(best(n)[:, eight], values(n))
                                elif what == 1:
                                    last = dve.max_index(places(n)[:, eight], best(n)[:, eight], values(n))
                                else:
                                    last = dve.match_replace(values(n), best(n)[:, eight], values(n), NEG)
                            done(last)

                dve.wait_ge(s_done, m + 1)
                r = rq[:, bass.ds(t, 1), :].rearrange("p a h -> p (a h)")
                dve.tensor_tensor(s_sb[:].rearrange("p (h two) n -> p h (two n)", two=2),
                                  ps[:, 2:6, :].rearrange("p b (h n) -> p (b h) n", h=2),
                                  bcast(r, [P, PH, 2 * NK], 2), ALU.mult).then_inc(s_out, 1)
                dve.wait_ge(s_out, m + 1)
                top16(2 * PH, lambda n: s_sb[:, n, :], lambda n: v12[:, n, :], lambda n: i12u[:, n, :])
                v = v12[:].rearrange("p (h two) k -> p h two k", two=2)
                shape = [P, PH, TOPK, TOPK]
                done(dve.tensor_tensor(cand[:], bcast(v[:, :, 0, :], shape, 3), bcast(v[:, :, 1, :], shape, 2), ALU.add))
                flat = cand[:].rearrange("p h a b -> p h (a b)")
                top16(PH, lambda n: flat[:, n, :], lambda n: tv[:, n, :], lambda n: tpos[:, n, :])
                done(dve.tensor_tensor(gate_e[:], tv[:], tv[:, :, 0:1].broadcast_to([P, PH, TOPK]), ALU.subtract))
                dve.tensor_copy(i12f[:], i12u[:]).then_inc(sm_sub, 1)
                pos = tpos[:].rearrange("p h k -> p (h k)")
                dve.tensor_scalar(posu[:, 0, :], pos, 4, None, ALU.logical_shift_right)
                done(dve.tensor_scalar(posu[:, 1, :], pos, 15, None, ALU.bitwise_and))
                done(dve.tensor_copy(posf[:], posu[:]))
                full = [P, PH * TOPK, TOPK]
                idx = i12f[:].rearrange("p (h two) a -> p h two a", two=2)
                eq4 = eq[:].rearrange("p (h k) a -> p h k a", h=PH)
                for j in range(2):
                    done(dve.tensor_tensor(eq[:], bcast(iota16[:], full, 1), bcast(posf[:, j, :], full, 2),
                                           ALU.is_equal))
                    done(dve.tensor_tensor(eq4, eq4, bcast(idx[:, :, j, :], [P, PH, TOPK, TOPK], 2), ALU.mult))
                    done(dve.tensor_reduce(sel[:, j, :], eq[:], AX_X, ALU.add))
                dve.wait_ge(sm_exp, m + 1)
                done(dve.tensor_reduce(gate_s[:, 0, :], gate_e[:], AX_X, ALU.add))
                done(dve.reciprocal(gate_s[:, 1, :], gate_s[:, 0, :]))
                dst = gate_far[:] if far else sel[:, 2, :]
                dve.tensor_tensor(dst.rearrange("p (h k) -> p h k", h=PH), gate_e[:],
                                  bcast(gate_s[:, 1, :], [P, PH, TOPK], 2), ALU.mult)\
                   .then_inc(far_sel if far else sel_made, 1)
                if far:
                    dve.scalar_tensor_tensor(out=idx_far[:], in0=sel[:, 0, :], scalar=float(NK), in1=sel[:, 1, :],
                                             op0=ALU.mult, op1=ALU.add).then_inc(far_sel, 1)
                    dve.wait_ge(far_sel, 2)
                else:
                    dve.wait_ge(sel_turned, t + 1)
                    dve.tensor_copy(selT[:, :, bass.ds(t * P, P)],
                                    ps[:, 6, 0:3 * P].rearrange("p (s n) -> p s n", s=3)).then_inc(selT_out, 1)
                assert step[0] == STEPS

            with dve.Fori(0, 1) as m:
                retrieve(m, m + FAR, True)
            with dve.Fori(0, NT) as t:
                retrieve(t + 1, t, False)
            dve.wait_ge(selT_out, NT)

            def hot(b, j):
                dve.wait_ge(g_mm, 16 * b + (j + 1))
                for q in range(4):
                    m = 4 * (j % 4) + q
                    tok = bass.ds(GSTEP * b + (4 * j + q), 1)
                    dve.tensor_scalar(hot_a[:, m, :], iota[:], selT[:, 0, tok], selT[:, 2, tok],
                                      ALU.is_equal, ALU.mult)
                    last = dve.tensor_scalar(hot_b[:, m, :], iota[:], selT[:, 1, tok], None, ALU.is_equal)
                last.then_inc(hot_made, 1)

            with dve.Fori(0, NEAR // GSTEP) as b:
                for j in range(16):
                    hot(b, j)

            blocks = "p (k c) -> p k c"

            def gate(i, par, c, src, use):
                dve.wait_ge(g_loaded[c], 16 * use)
                dve.tensor_tensor(src, src, gch[c], ALU.mult).then_inc(act_made, 1)
                dve.wait_ge(ahi_made, i + 1)
                dst = a_lo[par][:, c, :].rearrange("p (b t) -> p b t", t=P)
                dve.tensor_tensor(dst, src, a_hi[:, par, c, :].bitcast(F32).rearrange("p (b t) -> p b t", t=P),
                                  ALU.subtract).then_inc(alo_made, 1)

            def add_out(p, c):
                dve.wait_ge(ring_free, p + (1 + RING_SLOTS))
                for t in range(NT):
                    col = x1[:, t, c * BANK:(c + 1) * BANK]
                    dve.tensor_tensor(col, ps[:, 2 + 3 * (c % 2) + t, :], col, ALU.add).then_inc(y_added, 1)

            def use_rows(parts, part, q, b):
                n = sum(len(x) for x in parts[:part])
                for kind, batch, slot in parts[part]:
                    buf, col = n % GATHER_BUFS, BATCH * batch + slot
                    row = rows[buf][:]
                    if kind == "v" and slot == 0:
                        cols = a_far[:, BATCH * batch:BATCH * (batch + 1)]
                        dve.wait_ge(far_gelu, b + (batch + 1))
                        dve.tensor_tensor(cols, cols, gate_far[:, bass.ds(BATCH * b + BATCH * batch, BATCH)], ALU.mult)\
                           .then_inc(far_weight, 1)
                        dve.wait_ge(far_weight, b + (batch + 1))
                    gath = (q + (n - buf)) * (16 // GATHER_BUFS) + 16
                    if kind == "u":
                        dve.wait_ge(gathered[buf], gath)
                        row = row.rearrange(blocks, c=P)
                        dve.tensor_tensor_reduce(out=row, in0=row, in1=h_far, scale=1.0, scalar=0.0, op0=ALU.mult,
                                                 op1=ALU.add, accum_out=z_far[:, col:col + 1]).then_inc(row_used, 1)
                    else:
                        dve.wait_ge(row_used, q + (n + GATHER_BUFS))
                        dve.wait_ge(gathered[buf], gath)
                        dve.scalar_tensor_tensor(out=x1[:, FAR, :], in0=row, scalar=a_far[:, col:col + 1],
                                                 in1=x1[:, FAR, :], op0=ALU.mult, op1=ALU.add).then_inc(row_used, 1)
                    n += 1

            def down_group(g, par, part, parts, q, b):
                for c in range(GROUP):
                    p = 4 * g + (c + P_DOWN - GROUP)
                    make_lo(p + 1, (c + 1) % 2)
                    dve.wait_ge(gin_loaded[c % 2], 32 * g + (16 * (c // 2) + 16))
                    gate(4 * g + c, par, c, g_in[c % 2], g + 1)
                    use_rows(parts, part + c, q, b)
                    add_out(p, c)

            def both_group(g, par, part, q, b):
                for c in range(GROUP):
                    p = 8 * g + (2 * c + P_BOTH - 8 * PRE_GROUPS)
                    make_lo(p + 1, 1)
                    use_rows(BOTH_GATHERS, part + c, q, b)
                    make_lo(p + 2, 0)
                    dve.wait_ge(gelu_made, 4 * g + (c + 3))
                    gate(4 * g + c, par, c, gelu[:, c % 2, :].rearrange("p (b t) -> p b t", t=P), g + 1)
                    add_out(p + 1, c)

            for c in range(GROUP):
                dve.wait_ge(gin_loaded[c % 2], 16 * (c // 2) + 16)
                gate(c, 0, c, g_in[c % 2], 1)
            for b in range(2):
                dve.wait_ge(ahead_stored[b], 16 * (PRE // 2) + 16)
            dve.wait_ge(nf_loaded, 16)
            dve.scalar_tensor_tensor(out=h_far, in0=x1[:, FAR, :].rearrange(blocks, c=P), scalar=ss[:, FAR:FAR + 1],
                                     in1=rows[0][:].rearrange(blocks, c=P), op0=ALU.mult, op1=ALU.mult)\
               .then_inc(h_far_made, 1)
            dve.wait_ge(h_far_made, 1)
            dve.wait_ge(lo_made, P_DOWN + 1)
            with dve.Fori(0, PRE_GROUPS // 2 - 1) as r:
                down_group(2 * r + 1, 1, 0, DOWN_GATHERS, 8 * r, r)
                down_group(2 * r + 2, 0, 4, DOWN_GATHERS, 8 * r, r)
            with dve.Fori(PRE_GROUPS - 1, PRE_GROUPS) as g:
                down_group(g, 1, 0, TAIL_GATHERS, 8 * g - 8 * (PRE_GROUPS - 1) + 4 * PRE_GROUPS - 8,
                           g - (PRE_GROUPS - 1) + (PRE_GROUPS // 2 - 1))
            with dve.Fori(0, (N_GROUPS - PRE_GROUPS) // 2) as r:
                q, b = 24 * r + 4 * PRE_GROUPS, 3 * r + PRE_GROUPS // 2
                both_group(2 * r + PRE_GROUPS, 0, 0, q, b)
                both_group(2 * r + (PRE_GROUPS + 1), 1, 4, q, b)
            for c in range(GROUP):
                if c:
                    make_lo(P_LAST + c, c % 2)
                add_out(P_LAST + c, c)

        @block.tensor
        def _(pe):
            def three(dst, w_h, w_l, m_h, m_l, first, last):
                pe.matmul(dst, w_h, m_h, start=first, stop=False)
                pe.matmul(dst, w_h, m_l, start=False, stop=False)
                return pe.matmul(dst, w_l, m_h, start=False, stop=last)

            def turn(stage, sources):
                pe.wait_ge(normed[stage], sources)
                for k in range(KD):
                    if k >= NBANK:
                        pe.wait_ge(t_lo[stage], k - NBANK + 1)
                    for t in range(TT):
                        last = pe.transpose(ps[:, k % NBANK, t * P:(t + 1) * P], turned_from(stage, t, k), ident[:])
                    last.then_inc(turned[stage], 1)
                pe.wait_ge(t_lo[stage], KD)

            def rows_piece(p, slot, kq, bank):
                pe.wait_ge(lo_made, p + 1)
                for kk in range(4):
                    k = 4 * kq + kk
                    cols = slice(kk * BANK, (kk + 1) * BANK)
                    for t in range(TT):
                        a = slice(t * P, (t + 1) * P)
                        last = three(ps[:, bank + t, :], actT_hi[:, k, a], actT_lo[:, k, a],
                                     hi[:, slot, cols], lo[:, slot, cols], k == 0, k == KD - 1)
                last.then_inc(ring_free, 1)
                return last

            pe.sem_inc(ring_free, RING_SLOTS)
            pe.sem_inc(squared, 8)
            pe.wait_ge(s_const, 10)
            turn(IN_NORM, TT)
            with pe.Fori(0, PARTS) as i:
                for cc in range(2):
                    pe.wait_ge(squared, 8 * i + (4 * cc + 4))
                    for kq in range(KQ):
                        rows_piece(8 * i + (4 * cc + kq), kq % 2, kq, 4 * cc)

            pe.wait_ge(s_sgm, 1)
            pe.wait_ge(squared, 8 + 4 * IN_CHUNKS)
            for h in range(HEADS):
                pe.wait_ge(vb_made, TT * (h + 1))
                pe.matmul(ps[:, h, :], sgw_s[:, h, :], proj[:, G_PART, :, h * HD:(h + 1) * HD],
                          start=True, stop=True).then_inc(mixed, 1)

            Z_AT = ((0, 0), (1, 0), (2, 0), (1, 384))
            pe.wait_ge(gated, HEADS)
            pe.sem_inc(y_out, 1)
            with pe.Fori(0, HEADS // 2) as i:
                pe.wait_ge(y_out, 2 * i + 1)
                for ab in range(2):
                    n = 2 * i + ab
                    for j in range(2):
                        pe.wait_ge(qk_normed, 2 * n + (j + 1))
                        if ab:
                            pe.wait_ge(qkT_out, 4 * i + (j + 1))
                        for t in range(TT):
                            last = pe.transpose(ps[:, 7 * j, t * P:(t + 1) * P], qk_n[:, ab, j, t, :], ident[:])
                        last.then_inc(qk_turned, 1)
                for ab in range(2):
                    n = 2 * i + ab
                    pe.wait_ge(qkT_out, 2 * n + 2)
                    for b in range(TT):
                        bank, col = Z_AT[b]
                        last = pe.matmul(ps[:, 1 + 3 * ab + bank, col:col + SEQ - b * P],
                                         qkT[:, ab, 1, b * P:(b + 1) * P], qkT[:, ab, 0, b * P:SEQ],
                                         start=(b < 3), stop=True, skip_group_check=True)
                    last.then_inc(z_done, 1)
                for ab in range(2):
                    n = 2 * i + ab
                    pe.wait_ge(sp_kept, 2 * n + 2)
                    for b in range(TT):
                        bank, col = Z_AT[b]
                        for b2 in range(b, TT):
                            bank2, col2 = Z_AT[b2]
                            width = SEQ - b2 * P
                            at2 = bank2 * BANK + col2
                            off = col + (b2 - b) * P
                            last = pe.matmul(ps[:, 1 + 3 * ab + bank, off:off + width],
                                             tri[:] if b2 == b else neg1[:], sp[:, ab, at2:at2 + width],
                                             start=False, stop=True, skip_group_check=True)
                    last.then_inc(tails, 1)
                for ab in range(2):
                    n = 2 * i + ab
                    pe.wait_ge(w_made, n + 1)
                    pe.wait_ge(v_copied, n + 1)
                    if not ab:
                        pe.wait_ge(qkT_out, 4 * i + 4)
                    for t in range(TT):
                        for b in range(t + 1):
                            bank, col = Z_AT[b]
                            at1 = bank * BANK + col + (t - b) * P
                            last = pe.matmul(ps[:, 7 * ab, t * P:(t + 1) * P], w_att[:, ab, at1:at1 + P],
                                             v_h[:, ab, b, :], start=(t == 0 and b == 0), stop=(b == t),
                                             skip_group_check=True)
                    last.then_inc(pv_done, 1)

            turn(MIX_NORM, 2 * TT)
            pe.sem_inc(out_added, 8)
            with pe.Fori(0, 2) as i:
                for cc in range(2):
                    pe.wait_ge(out_added, 8 * i + (4 * cc + 4))
                    for kq in range(KQ):
                        rows_piece(8 * i + (P_OUT + 4 * cc + kq), kq % 2, kq, 4 * cc)
            turn(FFN_NORM, TT)

            for c in range(4):
                if c >= 2:
                    pe.wait_ge(q_out, 4 * (c - 1))
                    pe.wait_ge(q_sq, 4 * (c - 1))
                for kq in range(KQ):
                    m = 4 * c + kq
                    pe.wait_ge(lo_made, P_QUERY + m + 1)
                    for kk in range(4):
                        k = 4 * kq + kk
                        for b in range(4):
                            col = slice(kk * BANK + b * P, kk * BANK + (b + 1) * P)
                            last = three(ps[:, 4 * (c % 2) + b, :], hi[:, m % 2, col], lo[:, m % 2, col],
                                         actT_hi[:, k, :], actT_lo[:, k, :], k == 0, k == KD - 1)
                    last.then_inc(ring_free, 1)
            pe.wait_ge(q_pair, PH)
            pe.wait_ge(q_out, 16)
            for t in range(TT):
                for h in range(PH):
                    col = t * PH + h
                    last = pe.matmul(ps[:, 0, col:col + 1], sqh[:, h, t * P:(t + 1) * P], neg1[:, 0:1],
                                     start=True, stop=True)
            last.then_inc(q_ss, 1)
            pe.wait_ge(q_var, 1)

            def up(p, slot, i, z_bank):
                pe.wait_ge(gelu_made, i + 1)
                pe.wait_ge(lo_made, p + 1)
                for k in range(KD):
                    e = slice(k * P, (k + 1) * P)
                    last = three(ps[:, z_bank, 0:NEAR], hi[:, slot, e], lo[:, slot, e], actT_hi[:, k, 0:NEAR],
                                 actT_lo[:, k, 0:NEAR], k == 0, k == KD - 1)
                last.then_inc(ring_free, 1)

            def scores(m, t):
                if m:
                    pe.wait_ge(s_out, m)
                for n in range(2 * PH):
                    last = pe.matmul(ps[:, 2 + n // 4, (n % 4) * NK:(n % 4 + 1) * NK], qT[:, n, t * P:(t + 1) * P],
                                     keysT[:, n % 2, :], start=True, stop=True)
                last.then_inc(s_done, 1)

            pe.sem_inc(gelu_made, 2)
            pe.sem_inc(g_mm, 4)
            pe.sem_inc(g_out, 4)
            pe.sem_inc(y_added, 6)
            pe.sem_inc(row_used, GATHER_BUFS)

            def up_pairs(first, end):
                with pe.Fori(first, end) as h:
                    for b in range(2):
                        up(2 * h + (P_PEER + b), b, 2 * h + b, b)

            scores(0, FAR)
            up_pairs(0, AHEAD_FAR // 2)
            scores(1, 0)
            first = AHEAD_FAR // 2
            for t in range(NT):
                up_pairs(first, first + AHEAD_NEAR[t] // 2)
                first += AHEAD_NEAR[t] // 2
                if t + 1 < NT:
                    scores(t + 2, t + 1)
                pe.wait_ge(sel_made, t + 1)
                if t:
                    pe.wait_ge(selT_out, t)
                for j in range(3):
                    last = pe.transpose(ps[:, 6, j * P:(j + 1) * P], sel[:, j, :], ident[:])
                last.then_inc(sel_turned, 1)

            def outers(b, quad):
                for j in range(4 * quad, 4 * quad + 4):
                    pe.wait_ge(hot_made, 16 * b + (j + 1))
                    pe.wait_ge(g_out, 16 * b + (j + 1))
                    for q in range(4):
                        m = 4 * (j % 4) + q
                        last = pe.matmul(ps[:, 2 + j % 4, q * NK:(q + 1) * NK], hot_b[:, m, :], hot_a[:, m, :],
                                         start=True, stop=True)
                    last.then_inc(g_mm, 1)

            with pe.Fori(0, NEAR // GSTEP // 2) as r:
                for s in range(2):
                    b = 2 * r + s

                    def up_of(n):
                        at = AHEAD_1 + AHEAD_GATES // 2 * s + n
                        up(AHEAD_GATES * r + (at + P_PEER), at % 2, AHEAD_GATES * r + at, at % 2)

                    up_of(0)
                    outers(b, 0)
                    up_of(1)
                    for quad in range(1, 4):
                        up_of(quad + 1)
                        outers(b, quad)
            up_pairs(AHEAD_2 // 2, PRE // 2)
            pe.wait_ge(g_out, 4 + NEAR // 4)

            def down(p, slot, g, c, par):
                pe.wait_ge(lo_made, p + 1)
                if c == 0:
                    pe.wait_ge(alo_made, 4 * g + 4)
                pe.wait_ge(y_added, 12 * g + (3 * c + 3))
                for e in range(GROUP):
                    cols = slice(e * BANK, (e + 1) * BANK)
                    for t in range(NT):
                        a = slice(t * P, (t + 1) * P)
                        last = three(ps[:, 2 + 3 * (c % 2) + t, :], a_hi[:, par, e, a], a_lo[par][:, e, a],
                                     hi[:, slot, cols], lo[:, slot, cols], e == 0, e == GROUP - 1)
                last.then_inc(ring_free, 1)

            def down_group(g, par):
                for c in range(GROUP):
                    down(4 * g + (c + P_DOWN - GROUP), c % 2, g - 1, c, 1 - par)

            def both_group(g, par):
                for c in range(GROUP):
                    p = 8 * g + (2 * c + P_BOTH - 8 * PRE_GROUPS)
                    up(p, 0, 4 * g + c, c % 2)
                    down(p + 1, 1, g - 1, c, 1 - par)

            with pe.Fori(0, PRE_GROUPS // 2 - 1) as r:
                down_group(2 * r + 1, 1)
                down_group(2 * r + 2, 0)
            down_group(PRE_GROUPS - 1, 1)
            with pe.Fori(0, (N_GROUPS - PRE_GROUPS) // 2) as r:
                both_group(2 * r + PRE_GROUPS, 0)
                both_group(2 * r + (PRE_GROUPS + 1), 1)
            for c in range(GROUP):
                down(P_LAST + c, c % 2, N_GROUPS - 1, c, 1)


def kernel(x, norm_mix, w_in, q_norm, k_norm, sg_norm, sg_w, sg_b, out_norm_sb, out_norm_sg,
           w_out, norm_ffn, peer_w_query, peer_sub_keys, peer_u, peer_v):
    import numpy as np
    import concourse.bacc as bacc
    from concourse.bass_utils import run_bass_kernel_spmd

    def laid(a, *axes):
        return np.ascontiguousarray(np.transpose(a, axes) if axes else a)

    def pieces(w):
        n = w.shape[1] // BANK
        return laid(np.reshape(w, (KQ, 4, P, n, BANK)), 3, 0, 2, 1, 4).reshape(n * KQ, P, PIECE)

    def by_block(g):
        return laid(np.reshape(g, (-1, P)), 1, 0)

    f = np.asarray
    arrays = {
        "x": laid(f(x)[0]),
        "norm_mix": by_block(f(norm_mix)[0]),
        "norm_ffn": by_block(f(norm_ffn)[0]),
        "norm_y": by_block(np.concatenate([f(out_norm_sb)[0], f(out_norm_sg)[0]])),
        "q_norm": laid(f(q_norm)[0].reshape(P, 1)),
        "k_norm": laid(f(k_norm)[0].reshape(P, 1)),
        "sg_norm": laid(np.broadcast_to(f(sg_norm)[0].reshape(1, WIDTH), (P, WIDTH))),
        "sg_w": laid(f(sg_w)[0], 2, 0, 1),
        "sg_b": laid(f(sg_b)[0], 1, 0),
        "keys": laid(f(peer_sub_keys)[0], 2, 0, 1),
        "w_in": pieces(f(w_in)[0]),
        "w_out": pieces(f(w_out)[0]),
        "w_query": pieces(f(peer_w_query)[0]),
        "peer_u": laid(np.reshape(f(peer_u)[0], (NK, P, KD, P)), 0, 3, 2, 1).reshape(NK, P, PIECE),
        "peer_u_rows": laid(f(peer_u)[0]),
        "peer_v": laid(f(peer_v)[0]),
        "norm_ffn_rows": laid(np.broadcast_to(f(norm_ffn)[0].reshape(1, D), (P, D))),
    }
    nc = bacc.Bacc("TRN2", target_bir_lowering=False, num_devices=1)
    args = [nc.dram_tensor(n, a.shape, mybir.dt.from_np(a.dtype), kind="ExternalInput").ap()
            for n, a in arrays.items()]
    out = nc.dram_tensor("y", (SEQ, D), F32, kind="ExternalOutput").ap()
    layer(nc, *args, out)
    r = run_bass_kernel_spmd(nc, [arrays], core_ids=[0])
    return r.results[0]["y"].reshape(1, SEQ, D)
```

```python
from contextlib import ExitStack

import concourse.bass as bass
from concourse import mybir

ALU = mybir.AluOpType
ACT = mybir.ActivationFunctionType
AX_X = mybir.AxisListType.X
F32 = mybir.dt.float32
F32R = mybir.dt.float32r
U32 = mybir.dt.uint32

P = 128
SEQ = 512
TT = SEQ // P
D = 2048
KD = D // P
HEADS = 8
HD = 128
WIDTH = HEADS * HD
PARTS = 5
Q_PART, K_PART, V_PART, U_PART, G_PART = range(PARTS)
NBANK = 8
BANK = 512
EPS = 1e-6
BIG = 1.0e30

PH = 8
NK = 128
TOPK = 16
NEG = -3.0e38

PIECE = 2048
KQ = 4
IN_CHUNKS = PARTS * WIDTH // BANK
IN_PIECES = IN_CHUNKS * KQ
MM_PIECES = D // BANK * KQ
P_OUT = IN_PIECES
P_QUERY = P_OUT + MM_PIECES
P_PEER = P_QUERY + MM_PIECES
GROUP = 4
N_GROUPS = NK // GROUP
NEAR = SEQ - P
NT = NEAR // P
FAR = TT - 1
PRE = 64
PRE_GROUPS = PRE // GROUP
P_DOWN = P_PEER + PRE
P_BOTH = P_DOWN + GROUP * (PRE_GROUPS - 1)
P_LAST = P_BOTH + 2 * GROUP * (N_GROUPS - PRE_GROUPS)
GSTEP = 64
G_PARTS = 4
G_ALL = 16 * G_PARTS * (NEAR // GSTEP + 1)
RING_SLOTS = 2
SCALE = float(HD) ** -0.5
AHEAD_FAR, AHEAD_NEAR, AHEAD_GATES, AHEAD_TAIL = 8, (8, 6, 6), 5, 6
AHEAD_1 = AHEAD_FAR + sum(AHEAD_NEAR)
AHEAD_2 = AHEAD_1 + AHEAD_GATES * (NEAR // GSTEP)
assert AHEAD_2 + AHEAD_TAIL == PRE

IN_NORM, MIX_NORM, FFN_NORM = range(3)

BATCH = 4
GATHER_BUFS = 4


def steps(text):
    return [[(x[0], int(x[1]), int(x[2])) for x in part.split()] for part in text.split("|")]


DOWN_GATHERS = steps("u00 | u01 | u02 | u03 | v00 | v01 | v02 | v03")
DOWN_GELUS = {4: 0}
TAIL_GATHERS = steps("u00 u01 | u02 u03 | v00 v01 | v02 v03")
TAIL_GELUS = {2: 0}
BOTH_GATHERS = steps("u00 u01 u02 | u03 u10 u11 | v00 v01 v02 | v03 u12 u13 | u20 u21 u22 | u23 v10 v11 |"
                     " v12 v13 v20 | v21 v22 v23")
BOTH_GELUS = {2: 0, 4: 1, 6: 2}


def layer(nc, x, nm, nf, ny, qn, kn, sgn, sgw, sgb, keys, w_in, w_out, w_q, pu, u_rows, pv, nf_row, out):
    gates = nc.dram_tensor("gates_scratch", (NK // 2, NK, NEAR // GSTEP, 2, GSTEP), F32).ap()
    spill = nc.dram_tensor("gelu_scratch", (PRE, P, NEAR), F32).ap()

    base = [16512]

    def at(name, shape, dt, kb):
        return nc.alloc_sbuf_tensor_at(name, shape, dt, offset=base[0] + int(kb * 1024))

    actT_hi = at("actT_hi", [P, KD, SEQ], F32R, 0)
    actT_lo = at("actT_lo", [P, KD, SEQ], F32R, 32)
    raw = at("ring_raw", [P, RING_SLOTS, PIECE], F32, 64)
    hi = at("ring_hi", [P, RING_SLOTS, PIECE], F32R, 80)
    lo = at("ring_lo", [P, RING_SLOTS, PIECE], F32R, 96)
    proj = at("proj", [P, PARTS, TT, WIDTH], F32, 112)
    x0 = at("x0", [P, TT, D], F32, 112)
    junk0 = at("junk0", [P, D], F32, 160)
    qk_n = at("qk_n", [P, 2, 2, TT, HD], F32, 0)
    qkT = at("qkT", [P, 2, 2, SEQ], F32, 8)
    v_h = at("v_h", [P, 2, TT, HD], F32, 16)
    sp_t = at("sp_t", [P, 2, 1280], F32, 20)
    sp = at("sp", [P, 2, 1280], F32, 30)
    w_att = at("w_att", [P, 2, 1280], F32, 40)
    x1 = at("x1", [P, TT, D], F32, 128)
    junk1 = at("junk1", [P, D], F32, 176)
    junk2 = at("junk2", [P, D], F32, 112)
    sqh = at("sqh", [P, PH, SEQ], F32, 112)
    qT = at("qT", [P, 2 * PH, SEQ], F32, 160)
    s_sb = at("s_sb", [P, 2 * PH, NK], F32, 112)
    eq = at("eq", [P, PH * TOPK, TOPK], F32, 112)
    cand = at("cand", [P, PH, TOPK, TOPK], F32, 120)
    posu = at("posu", [P, 2, PH * TOPK], U32, 120)
    posf = at("posf", [P, 2, PH * TOPK], F32, 121)
    gate_e = at("gate_e", [P, PH, TOPK], F32, 122)
    sel = at("sel", [P, 3, P], F32, 122.5)
    i12f = at("i12f", [P, 2 * PH, TOPK], F32, 124)
    v12 = at("v12", [P, 2 * PH, TOPK], F32, 196)
    i12u = at("i12u", [P, 2 * PH, TOPK], U32, 197)
    tv = at("tv", [P, PH, TOPK], F32, 198)
    tpos = at("tpos", [P, PH, TOPK], U32, 198.5)
    gate_s = at("gate_s", [P, 2, PH], F32, 199)
    gbuf = at("gbuf", [P, NK, GSTEP], F32, 160)
    hot_a = at("hot_a", [P, 16, NK], F32, 112)
    hot_b = at("hot_b", [P, 16, NK], F32, 120)
    free_hi = at("free_hi", [P, KD, SEQ], F32, 0)[:, :, NEAR:SEQ]
    free_lo = at("free_lo", [P, KD, SEQ], F32, 32)[:, :, NEAR:SEQ]
    ahead = [free_hi[:, 3 * b:3 * b + 3, :] for b in range(2)]
    h_far = free_hi
    g_pair = [free_lo[:, 6 * q:6 * q + 6, :] for q in range(GROUP // 2)]
    gelu = at("gelu", [P, 2, NEAR], F32, 124)
    g_in = [free_lo[:, 12:15, :], at("g_in_1", [P, NT, P], F32, 190)[:]]
    a_hi = at("a_hi", [P, 2, GROUP, NEAR], F32R, 112)
    a_lo = [at("a_lo_0", [P, GROUP, NEAR], F32R, 200), at("a_lo_1", [P, GROUP, NEAR], F32R, 184)]
    rows = [at(f"rows_{b}", [P, D], F32, kb) for b, kb in enumerate((160, 168, 176, 192))]
    ident = at("ident", [P, P], F32, 192)
    tri = at("tri", [P, P], F32, 192.5)
    neg1 = at("neg1", [P, P], F32, 193)
    keep = at("keep", [P, P], F32, 193.5)
    block_m = at("block_m", [P, P], F32, 194)
    iota = at("iota128", [P, NK], F32, 194.5)
    keysT = at("keysT", [P, 2, NK], F32, 195)
    sq = at("sq", [P, 2, BANK], F32, 196)
    diag = at("diag", [P, 2 * TT, P], F32, 196)
    selT = at("selT", [P, 3, NEAR], F32, 200)
    iota16 = at("iota16", [P, TOPK], F32, 206)
    small = at("small", [P, 110], F32, 206.0625)
    stats = at("stats", [P, PARTS, TT, HEADS], F32, 206.5)
    gains = small[:, 0:48].rearrange("p (s k) -> p s k", s=3)
    qgain, kgain, sgb_s = small[:, 48:49], small[:, 49:50], small[:, 50:58]
    ss = small[:, 58:66]
    rq = small[:, 66:98].rearrange("p (t h) -> p t h", t=TT)
    ss_part = small[:, 66:82].rearrange("p (t c) -> p t c", t=TT)
    tick, pool_ticks = small[:, 98:99], small[:, 99:101]
    idx_far = at("idx_far", [P, P], U32, 206.5)
    z_far = at("z_far", [P, 3 * BATCH], F32, 207)
    a_far = at("a_far", [P, 3 * BATCH], F32, 207.0625)
    idx_now = at("idx_now", [P, GATHER_BUFS], U32, 207.125)
    gate_far = at("gate_far", [P, P], F32, 207.25)
    sgw_s = at("sgw_s", [P, HEADS, P], F32, 52)
    sgn_s = at("sgn_s", [P, WIDTH], F32, 56)

    with ExitStack() as ctx:
        ps = ctx.enter_context(nc.psum_tensor("ps", [P, NBANK, BANK], F32))

        def sem(name):
            return ctx.enter_context(nc.semaphore(name))

        s_par = sem("params_loaded")
        s_x = [sem(f"x_loaded_{t}") for t in range(TT)]
        s_const = sem("constants_made")
        raw_full = [sem(f"raw_full_{s}") for s in range(RING_SLOTS)]
        hi_made = sem("hi_made")
        lo_made = sem("lo_made")
        ring_free = sem("ring_free")
        row_sq = [sem(f"row_squares_{s}") for s in range(3)]
        var_made = [sem(f"variance_{s}") for s in range(3)]
        rooted = [sem(f"rooted_{s}") for s in range(3)]
        inverted = [sem(f"inverted_{s}") for s in range(3)]
        normed = [sem(f"rows_normed_{s}") for s in range(3)]
        turned = [sem(f"turned_{s}") for s in range(3)]
        t_hi = [sem(f"turned_hi_{s}") for s in range(3)]
        t_lo = [sem(f"turned_lo_{s}") for s in range(3)]
        proj_out = sem("proj_copied_out")
        squared = sem("proj_squared")
        reduced = sem("proj_squares_reduced")
        st_var, st_root, st_inv = sem("stats_var"), sem("stats_rooted"), sem("stats_inverted")
        s_sgp = sem("gmlp_params_loaded")
        s_sgm = sem("gmlp_masked")
        vb_made, mixed, gated = sem("vb_made"), sem("mixed"), sem("gated")
        qk_normed, v_copied = sem("qk_normed"), sem("v_copied")
        qk_turned, qkT_out = sem("qk_turned"), sem("qkT_out")
        z_done, z_abs, z_exp, z_ln = sem("z_done"), sem("z_abs"), sem("z_exp"), sem("z_ln")
        sp_made, sp_kept = sem("sp_made"), sem("sp_kept")
        tails, z_blocked, w_made = sem("tails"), sem("z_blocked"), sem("w_made")
        pv_done, y_out = sem("pv_done"), sem("y_out")
        s_x1 = sem("x1_loaded")
        out_added = sem("out_added")
        q_out, q_sq, q_pair = sem("q_out"), sem("q_squared"), sem("q_pair_added")
        q_ss, q_var, q_root, q_inv = sem("q_ss"), sem("q_var"), sem("q_root"), sem("q_inv")
        s_done, s_out, topk, sm_sub, sm_exp = (sem("scores_done"), sem("scores_out"), sem("topk_step"),
                                               sem("softmax_sub"), sem("softmax_exp"))
        sel_made, sel_turned, selT_out = sem("sel_made"), sem("sel_turned"), sem("selT_out")
        hot_made, g_mm, g_out, g_stored = sem("hot_made"), sem("g_mm"), sem("g_out"), sem("g_stored")
        ahead_stored = [sem(f"ahead_stored_{b}") for b in range(2)]
        g_loaded = [sem(f"gates_loaded_{q}") for q in range(GROUP // 2)]
        gin_loaded = [sem(f"gelu_loaded_{b}") for b in range(2)]
        gelu_made, act_made, ahi_made, alo_made = (sem("gelu_made"), sem("act_made"), sem("a_hi_made"),
                                                   sem("a_lo_made"))
        y_added = sem("expert_y_added")
        far_sel, nf_loaded, h_far_made = sem("far_selected"), sem("norm_row_loaded"), sem("h_far_made")
        idx_copied = sem("idx_copied")
        gathered = [sem(f"gathered_{b}") for b in range(GATHER_BUFS)]
        row_used = sem("row_used")
        far_gelu, far_weight = sem("far_gelu"), sem("far_weight")
        s_stored = sem("out_stored")

        block = ctx.enter_context(nc.Block())

        def turned_from(stage, tt, k):
            if stage == IN_NORM:
                return x0[:, tt, k * P:(k + 1) * P], diag[:, tt, :]
            if stage == FFN_NORM:
                return x1[:, tt, k * P:(k + 1) * P], diag[:, tt, :]
            half, k = k // HEADS, k % HEADS
            return proj[:, (Q_PART, U_PART)[half], tt, k * P:(k + 1) * P], diag[:, half * TT + tt, :]

        def bcast(ap, shape, *axes):
            for a in axes:
                ap = ap.unsqueeze(a)
            return ap.broadcast_to(shape)

        @block.sync
        def _(sp_eng):
            for t in range(TT):
                sp_eng.dma_start(x0[:, t, :], x[t * P:(t + 1) * P, :]).then_inc(s_x[t], 16)

            def load(src, p, slot, n):
                sp_eng.wait_ge(lo_made, p - 1)
                sp_eng.dma_start(raw[:, slot, :], src[bass.ds(n, 1)].rearrange("a p n -> p (a n)"))\
                      .then_inc(raw_full[slot], 16)

            for p in range(RING_SLOTS):
                sp_eng.dma_start(raw[:, p, :], w_in[p]).then_inc(raw_full[p], 16)
            with sp_eng.Fori(1, IN_PIECES // 2) as i:
                for s in range(2):
                    load(w_in, 2 * i + s, s, 2 * i + s)
            for src, first in ((w_out, P_OUT), (w_q, P_QUERY)):
                with sp_eng.Fori(0, MM_PIECES // 2) as i:
                    for s in range(2):
                        load(src, 2 * i + s + first, s, 2 * i + s)
            with sp_eng.Fori(0, PRE // 2) as i:
                for s in range(2):
                    load(pu, 2 * i + s + P_PEER, s, 2 * i + s)

            def load_v(p, slot, g, c):
                sp_eng.wait_ge(lo_made, p - 1)
                src = pv.rearrange("(g el e) d -> g e el d", el=GROUP, e=P)[bass.ds(g, 1), :, :,
                                                                            c * BANK:(c + 1) * BANK]
                sp_eng.dma_start(raw[:, slot, :].rearrange("p (el d) -> p el d", el=GROUP),
                                 src.rearrange("g e el d -> e (g el) d")).then_inc(raw_full[slot], 16)

            def load_gates(n, q):
                sp_eng.dma_start(g_pair[q], gates[bass.ds(n, 1)].rearrange("a j b i t -> j (a b) (i t)"))\
                      .then_inc(g_loaded[q], 16)

            def load_gelu(i, b):
                sp_eng.dma_start(g_in[b], spill[bass.ds(i, 1)].rearrange("a e (b t) -> e (a b) t", t=P))\
                      .then_inc(gin_loaded[b], 16)

            load_v(P_DOWN, 0, 0, 0)
            sp_eng.wait_ge(g_stored, G_ALL)
            for b in range(2):
                sp_eng.wait_ge(ahead_stored[b], 16 * (GROUP // 2) + 16)
            for c in range(GROUP):
                if c % 2 == 0:
                    load_gates(c // 2, c // 2)
                if c >= 2:
                    sp_eng.wait_ge(alo_made, c - 1)
                load_gelu(c, c % 2)
            for b in range(2):
                sp_eng.wait_ge(ahead_stored[b], 16 * (PRE // 2) + 16)

            def down_group(g, last):
                for c in range(GROUP):
                    i = GROUP * g + c
                    if c < GROUP - 1:
                        load_v(4 * g + (c + P_DOWN - GROUP + 1), (c + 1) % 2, g - 1, c + 1)
                    elif not last:
                        load_v(4 * g + P_DOWN, 0, g, 0)
                    if c % 2 == 0:
                        sp_eng.wait_ge(act_made, i - 2)
                        load_gates(GROUP // 2 * g + c // 2, c // 2)
                    sp_eng.wait_ge(alo_made, i - 1)
                    load_gelu(i, c % 2)

            with sp_eng.Fori(1, PRE_GROUPS - 1) as g:
                down_group(g, False)
            with sp_eng.Fori(PRE_GROUPS - 1, PRE_GROUPS) as g:
                down_group(g, True)
            with sp_eng.Fori(PRE_GROUPS, N_GROUPS) as g:
                for c in range(GROUP):
                    p = 8 * g + (P_BOTH - 8 * PRE_GROUPS + 2 * c)
                    if c % 2 == 0:
                        sp_eng.wait_ge(act_made, GROUP * g + (c - 2))
                        load_gates(GROUP // 2 * g + c // 2, c // 2)
                    load(pu, p, 0, GROUP * g + c)
                    load_v(p + 1, 1, g - 1, c)
            for c in range(GROUP):
                load_v(P_LAST + c, c % 2, N_GROUPS - 1, c)
            sp_eng.wait_ge(row_used, 2 * P + GATHER_BUFS)
            sp_eng.dma_start(out[FAR * P:SEQ, :], x1[:, FAR, :]).then_inc(s_stored, 16)
            by_tile = out.rearrange("(t p) d -> p t d", p=P)
            for c in range(GROUP):
                cols = slice(c * BANK, (c + 1) * BANK)
                sp_eng.wait_ge(y_added, NT * GROUP * (N_GROUPS - 1) + NT * (c + 1) + 6)
                sp_eng.dma_start(by_tile[:, 0:NT, cols], x1[:, 0:NT, cols]).then_inc(s_stored, 16)
            sp_eng.wait_ge(s_stored, 16 * (GROUP + 1))

        @block.gpsimd
        def _(pool):
            made = [0]

            def const(ins):
                made[0] += 1
                ins.then_inc(s_const, 1)
                pool.wait_ge(s_const, made[0])

            for dst, src in ((gains[:, 0, :], nm), (gains[:, 1, :], ny), (gains[:, 2, :], nf), (qgain, qn),
                             (kgain, kn), (sgb_s, sgb), (keysT[:], keys)):
                pool.dma_start(dst, src).then_inc(s_par, 16)
            const(pool.memset(ident[:], 0.0))
            const(pool.affine_select(out=ident[:], in_=ident[:], compare_op=ALU.not_equal, fill=1.0, base=0,
                                     pattern=[[-1, P]], channel_multiplier=1))
            const(pool.memset(neg1[:], -1.0))
            const(pool.affine_select(out=tri[:], in_=neg1[:], compare_op=ALU.is_ge, fill=0.0, base=0,
                                     pattern=[[-1, P]], channel_multiplier=1))
            const(pool.memset(keep[:], 1.0))
            const(pool.affine_select(out=keep[:], in_=keep[:], compare_op=ALU.is_gt, fill=0.0, base=0,
                                     pattern=[[1, P]], channel_multiplier=-1))
            const(pool.memset(block_m[:], 0.0))
            const(pool.affine_select(out=block_m[:], in_=block_m[:], compare_op=ALU.is_gt, fill=-BIG, base=0,
                                     pattern=[[1, P]], channel_multiplier=-1))
            const(pool.iota(iota[:], [[1, NK]], base=0, channel_multiplier=0,
                            allow_small_or_imprecise_dtypes=True))
            const(pool.iota(iota16[:], [[1, TOPK]], base=0, channel_multiplier=0,
                            allow_small_or_imprecise_dtypes=True))
            pool.wait_ge(ring_free, RING_SLOTS + IN_PIECES)
            pool.dma_start(sgw_s[:], sgw).then_inc(s_sgp, 16)
            pool.dma_start(sgn_s[:], sgn).then_inc(s_sgp, 16)
            for i in range(HEADS // 2):
                if i:
                    pool.wait_ge(pv_done, 2 * i)
                for ab in range(2):
                    pool.wait_ge(proj_out, 4 * IN_CHUNKS)
                    pool.tensor_copy(v_h[:, ab, :, :], proj[:, V_PART, :, bass.ds((2 * i + ab) * HD, HD)])\
                        .then_inc(v_copied, 1)
            pool.wait_ge(pv_done, HEADS)
            pool.wait_ge(v_copied, HEADS)
            pool.dma_start(x1[:], x.rearrange("(t p) d -> p t d", p=P)).then_inc(s_x1, 16)

            pool.wait_ge(lo_made, P_PEER)

            def make_lo(p, slot):
                pool.wait_ge(hi_made, p + 1)
                pool.tensor_tensor(lo[:, slot, :], raw[:, slot, :], hi[:, slot, :].bitcast(F32), ALU.subtract)\
                    .then_inc(lo_made, 1)

            with pool.Fori(0, PRE // 2) as i:
                for s in range(2):
                    make_lo(2 * i + (P_PEER + s), s)
            make_lo(P_DOWN, 0)

            pool.wait_ge(g_stored, G_ALL)
            pool.dma_start(rows[0][:], nf_row).then_inc(nf_loaded, 16)
            pool.wait_ge(far_sel, 2)
            pool.wait_ge(h_far_made, 1)

            def carry(k):
                pool.tensor_tensor(pool_ticks[:, k:k + 1], kgain, kgain, ALU.add)

            def gather(parts, q, b):
                n = 0
                for part in parts:
                    for kind, batch, slot in part:
                        buf = n % GATHER_BUFS
                        pool.wait_ge(row_used, q + (n + 1))
                        carry(0)
                        pool.tensor_copy(idx_now[:, buf:buf + 1],
                                         idx_far[:, bass.ds(BATCH * b + (BATCH * batch + slot), 1)])\
                            .then_inc(idx_copied, 1)
                        pool.wait_ge(idx_copied, q + (n + 1))
                        carry(1)
                        pool.indirect_dma_start(
                            out=rows[buf][:], out_offset=None, in_=u_rows if kind == "u" else pv,
                            in_offset=bass.IndirectOffsetOnAxis(ap=idx_now[:, buf:buf + 1], axis=0))\
                            .then_inc(gathered[buf], 16)
                        n += 1

            with pool.Fori(0, PRE_GROUPS // 2 - 1) as r:
                gather(DOWN_GATHERS, 8 * r, r)
            with pool.Fori(0, 1) as r:
                gather(TAIL_GATHERS, 8 * r + 4 * PRE_GROUPS - 8, r + PRE_GROUPS // 2 - 1)
            with pool.Fori(0, (N_GROUPS - PRE_GROUPS) // 2) as r:
                gather(BOTH_GATHERS, 24 * r + 4 * PRE_GROUPS, 3 * r + PRE_GROUPS // 2)

        @block.scalar
        def _(act):
            def make_hi(p, slot, use):
                act.wait_ge(raw_full[slot], 16 * use)
                act.wait_ge(ring_free, p + 1)
                act.activation(hi[:, slot, :], raw[:, slot, :], ACT.Copy).then_inc(hi_made, 1)

            def root(stage, cols):
                act.wait_ge(var_made[stage], 1)
                act.activation(ss[:, 0:cols], ss[:, 0:cols], ACT.Sqrt).then_inc(rooted[stage], 1)

            def turn_hi(stage):
                for k in range(KD):
                    act.wait_ge(turned[stage], k + 1)
                    act.activation(actT_hi[:, k, :], ps[:, k % NBANK, :], ACT.Copy,
                                   scale=gains[:, stage, k:k + 1]).then_inc(t_hi[stage], 1)

            for t in range(TT):
                act.wait_ge(s_x[t], 16)
                act.activation(junk0[:], x0[:, t, :], ACT.Square, accum_out=ss[:, t:t + 1])\
                   .then_inc(row_sq[IN_NORM], 1)
                act.wait_ge(row_sq[IN_NORM], t + 1)
            root(IN_NORM, TT)
            act.wait_ge(s_par, 16 * 7)
            turn_hi(IN_NORM)

            def evac_in(c, i, part, cc, func):
                act.wait_ge(ring_free, 4 * c + (4 + RING_SLOTS))
                for t in range(TT):
                    dst = proj[:, bass.ds(part, 1), t, cc * BANK:(cc + 1) * BANK].rearrange("p a n -> p (a n)")
                    act.activation(dst, ps[:, cc * 4 + t, :], func).then_inc(proj_out, 1)
                    act.wait_ge(proj_out, 4 * c + t + 1)
                    act.wait_ge(reduced, 4 * c + t + 1)
                    act.activation(sq[:, t % 2, :], dst, ACT.Square).then_inc(squared, 1)

            act.sem_inc(reduced, 2)
            act.wait_ge(raw_full[0], 16)
            make_hi(0, 0, 1)
            for first, count, func in ((0, 3, ACT.Copy), (3, 2, ACT.Gelu)):
                for i in range(first, first + count):
                    for cc in range(2):
                        for kq in range(KQ):
                            n = 4 * cc + kq + 1
                            make_hi(8 * i + n, n % 2, 4 * i + n // 2 + 1)
                        evac_in(2 * i + cc, i, i, cc, func)
            act.wait_ge(st_var, 1)
            st = stats[:].rearrange("p a t h -> p (a t h)")
            act.activation(st, st, ACT.Sqrt).then_inc(st_root, 1)

            def copy_qk(n):
                for j, gain in ((0, qgain), (1, kgain)):
                    act.wait_ge(qk_turned, 2 * n + j + 1)
                    act.activation(qkT[:, n % 2, j, :], ps[:, 7 * j, :], ACT.Copy, scale=gain).then_inc(qkT_out, 1)

            def square_y(half, t, n):
                act.activation(junk1[:, 0:WIDTH], proj[:, (Q_PART, U_PART)[half], t, :], ACT.Square,
                               accum_out=ss[:, half * TT + t:half * TT + t + 1]).then_inc(row_sq[MIX_NORM], 1)
                act.wait_ge(row_sq[MIX_NORM], n + 1)

            copy_qk(0)
            copy_qk(1)
            for i in range(HEADS // 2):
                for ab in range(2):
                    n = 2 * i + ab
                    z = ps[:, 1 + 3 * ab:4 + 3 * ab, :].rearrange("p b n -> p (b n)")[:, 0:1280]
                    act.wait_ge(z_done, n + 1)
                    act.activation(sp_t[:, ab, :], z, ACT.Abs).then_inc(z_abs, 1)
                    act.wait_ge(z_abs, n + 1)
                    act.activation(sp_t[:, ab, :], sp_t[:, ab, :], ACT.Exp, scale=-1.0).then_inc(z_exp, 1)
                    act.wait_ge(z_exp, n + 1)
                    act.activation(sp_t[:, ab, :], sp_t[:, ab, :], ACT.Ln, bias=1.0).then_inc(z_ln, 1)
                    if n + 2 < HEADS:
                        copy_qk(n + 2)
                for ab in range(2):
                    n = 2 * i + ab
                    z = ps[:, 1 + 3 * ab:4 + 3 * ab, :].rearrange("p b n -> p (b n)")[:, 0:1280]
                    act.wait_ge(z_blocked, 2 * n + 2)
                    act.activation(w_att[:, ab, :], z, ACT.Exp).then_inc(w_made, 1)
                if i == 0:
                    act.wait_ge(gated, HEADS)
                square_y(1, i, i)
                for ab in range(2):
                    n = 2 * i + ab
                    act.wait_ge(pv_done, n + 1)
                    act.activation(proj[:, Q_PART, :, bass.ds(n * HD, HD)],
                                   ps[:, 7 * ab, :].rearrange("p (t c) -> p t c", t=TT), ACT.Copy)\
                       .then_inc(y_out, 1)

            act.wait_ge(y_out, HEADS + 1)
            for t in range(TT):
                square_y(0, t, TT + t)
            root(MIX_NORM, 2 * TT)
            turn_hi(MIX_NORM)
            for c in range(KQ):
                for kq in range(KQ):
                    n = 4 * c + kq + 1
                    make_hi(P_OUT + n, n % 2, (P_OUT + n) // 2 + 1)
                for cc in (c - 1, c) if c == KQ - 1 else (c - 1,):
                    for t in range(TT):
                        if cc < 0:
                            continue
                        n = TT * cc + t
                        act.wait_ge(out_added, 8 + n + 1)
                        act.activation(junk2[:, 0:BANK], x1[:, t, cc * BANK:(cc + 1) * BANK], ACT.Square,
                                       accum_out=ss_part[:, t, cc:cc + 1]).then_inc(row_sq[FFN_NORM], 1)
                        act.wait_ge(row_sq[FFN_NORM], n + 1)
            root(FFN_NORM, TT)
            turn_hi(FFN_NORM)

            for c in range(4):
                for kq in range(KQ):
                    m = 4 * c + kq + 1
                    make_hi(P_QUERY + m, m % 2, (P_QUERY + m) // 2 + 1)
                act.wait_ge(ring_free, P_QUERY + 4 * c + 4 + RING_SLOTS)
                for b in range(4):
                    m = 4 * c + b
                    act.activation(qT[:, m, :], ps[:, (c % 2) * 4 + b, :], ACT.Copy).then_inc(q_out, 1)
                    if m >= 2:
                        act.wait_ge(q_pair, m // 2)
                    act.activation(sq[:, b % 2, :], ps[:, (c % 2) * 4 + b, :], ACT.Square).then_inc(q_sq, 1)
                    if m == MM_PIECES - 2:
                        make_hi(P_PEER + 1, 1, P_PEER // 2 + 1)
            def ahead_tile(half, b, last=False):
                i, p = 2 * half + b, 2 * half + (b + P_PEER)
                act.wait_ge(ring_free, p + (1 + RING_SLOTS))
                act.wait_ge(ahead_stored[b], 16 * half + 16)
                act.activation(ahead[b], ps[:, b, 0:NEAR].rearrange("p (b t) -> p b t", t=P), ACT.Gelu)\
                   .then_inc(gelu_made, 1)
                if not last:
                    make_hi(p + 2, b, half + (P_PEER // 2 + 2))
                act.wait_ge(gelu_made, i + 3)
                act.dma_start(spill[bass.ds(i, 1)].rearrange("a e (b t) -> e (a b) t", t=P), ahead[b])\
                   .then_inc(ahead_stored[b], 16)

            for b in range(2):
                act.sem_inc(ahead_stored[b], 16)

            def softmax_exp(m):
                act.wait_ge(sm_sub, m + 1)
                act.activation(gate_e[:], gate_e[:], ACT.Exp).then_inc(sm_exp, 1)

            with act.Fori(0, 1) as h:
                for b in range(2):
                    ahead_tile(h, b)
            act.wait_ge(q_var, 1)
            act.activation(rq, rq, ACT.Sqrt).then_inc(q_root, 1)
            first = 2
            for m, count in enumerate((AHEAD_FAR - 2,) + AHEAD_NEAR):
                exp_at = first // 2 + (count // 2 - 1)
                with act.Fori(first // 2, exp_at) as h:
                    for b in range(2):
                        ahead_tile(h, b)
                softmax_exp(m)
                with act.Fori(exp_at, exp_at + 1) as h:
                    for b in range(2):
                        ahead_tile(h, b)
                first += count

            act.sem_inc(g_stored, 16 * G_PARTS)
            waited = act.alloc_register("waited")

            def copy_gates(b, quad):
                for j in range(4 * quad, 4 * quad + 4):
                    act.wait_ge(g_mm, 16 * b + (j + 1 + 4))
                    act.reg_mov(waited, 0)
                    act.activation(gbuf[:, :, 4 * j:4 * j + 4],
                                   ps[:, 2 + j % 4, :].rearrange("p (t i) -> p i t", t=4), ACT.Copy)\
                       .then_inc(g_out, 1)

            def store_gates(b, part):
                n = NK // 2 // G_PARTS
                dst = gates.rearrange("h j b i t -> j h b (i t)")[:, part * n:(part + 1) * n, bass.ds(b, 1), :]
                src = gbuf[:].rearrange("p (h i) t -> p h (i t)", i=2)[:, part * n:(part + 1) * n, :]
                act.dma_start(dst.rearrange("j h b n -> j h (b n)"), src).then_inc(g_stored, 16)

            with act.Fori(AHEAD_1 // 2, AHEAD_1 // 2 + 1) as h:
                for b in range(2):
                    ahead_tile(h, b)
            with act.Fori(0, NEAR // GSTEP // 2) as r:
                for s in range(2):
                    b = 2 * r + s

                    def ahead_of(n):
                        at = AHEAD_1 + AHEAD_GATES * s + n
                        ahead_tile(AHEAD_GATES * r + at // 2, at % 2)

                    act.wait_ge(g_stored, 16 * G_PARTS * b + 16 * G_PARTS)
                    act.reg_mov(waited, 0)
                    copy_gates(b, 0)
                    for quad in range(1, 4):
                        ahead_of(quad + 1)
                        copy_gates(b, quad)
                    act.wait_ge(g_out, 16 * b + (16 + 4))
                    store_gates(b, 0)
                    store_gates(b, 1)
                    for n in range(2):
                        ahead_of(AHEAD_GATES + n)
                        store_gates(b, 2 + n)

            def a_hi_of(i, par, c, src):
                act.wait_ge(act_made, i + 1)
                act.activation(a_hi[:, par, c, :].rearrange("p (b t) -> p b t", t=P), src, ACT.Copy)\
                   .then_inc(ahi_made, 1)

            with act.Fori(AHEAD_2 // 2 + 1, PRE // 2 - 1) as h:
                for b in range(2):
                    ahead_tile(h, b)
            with act.Fori(PRE // 2 - 1, PRE // 2) as h:
                ahead_tile(h, 0)
                a_hi_of(0, 0, 0, g_in[0])
                ahead_tile(h, 1, last=True)

            def gelu_far(gelus, parts, part, q):
                if part in gelus:
                    batch = gelus[part]
                    flat = [x for one in parts for x in one]
                    n = flat.index(("u", batch, BATCH - 1)) + 1
                    cols = slice(BATCH * batch, BATCH * (batch + 1))
                    act.wait_ge(row_used, q + (n + GATHER_BUFS))
                    act.activation(a_far[:, cols], z_far[:, cols], ACT.Gelu).then_inc(far_gelu, 1)

            def down_group(g, par, part, gelus, parts, q):
                for c in range(GROUP):
                    gelu_far(gelus, parts, part + c, q)
                    make_hi(4 * g + (c + P_DOWN - GROUP + 1), (c + 1) % 2,
                            2 * g + ((P_DOWN - GROUP) // 2 + (c + 1) // 2 + 1))
                    a_hi_of(4 * g + c, par, c, g_in[c % 2])

            def both_group(g, par, part, q):
                for c in range(GROUP):
                    p = 8 * g + (2 * c + P_BOTH - 8 * PRE_GROUPS)
                    use = 4 * g + (c + (P_BOTH - 8 * PRE_GROUPS) // 2 + 1)
                    gelu_far(BOTH_GELUS, BOTH_GATHERS, part + c, q)
                    make_hi(p + 1, 1, use)
                    make_hi(p + 2, 0, use + 1)
                    act.wait_ge(ring_free, p + (1 + RING_SLOTS))
                    act.wait_ge(alo_made, 4 * g + (c - 1))
                    act.activation(gelu[:, c % 2, :], ps[:, c % 2, 0:NEAR], ACT.Gelu).then_inc(gelu_made, 1)
                    a_hi_of(4 * g + c, par, c, gelu[:, c % 2, :].rearrange("p (b t) -> p b t", t=P))

            for c in range(1, GROUP):
                a_hi_of(c, 0, c, g_in[c % 2])
            with act.Fori(0, PRE_GROUPS // 2 - 1) as r:
                down_group(2 * r + 1, 1, 0, DOWN_GELUS, DOWN_GATHERS, 8 * r)
                down_group(2 * r + 2, 0, 4, DOWN_GELUS, DOWN_GATHERS, 8 * r)
            down_group(PRE_GROUPS - 1, 1, 0, TAIL_GELUS, TAIL_GATHERS, 4 * PRE_GROUPS - 8)
            with act.Fori(0, (N_GROUPS - PRE_GROUPS) // 2) as r:
                both_group(2 * r + PRE_GROUPS, 0, 0, 24 * r + 4 * PRE_GROUPS)
                both_group(2 * r + (PRE_GROUPS + 1), 1, 4, 24 * r + 4 * PRE_GROUPS)
            for c in range(1, GROUP):
                make_hi(P_LAST + c, c % 2, (P_LAST + c) // 2 + 1)

        @block.vector
        def _(dve):
            def make_lo(p, slot):
                dve.wait_ge(hi_made, p + 1)
                dve.tensor_tensor(lo[:, slot, :], raw[:, slot, :], hi[:, slot, :].bitcast(F32), ALU.subtract)\
                   .then_inc(lo_made, 1)

            def inverse_rms(stage, cols, width, n_sq):
                dve.wait_ge(row_sq[stage], n_sq)
                dve.tensor_scalar(ss[:, 0:cols], ss[:, 0:cols], 1.0 / width, EPS, ALU.mult, ALU.add)\
                   .then_inc(var_made[stage], 1)
                dve.wait_ge(rooted[stage], 1)
                dve.reciprocal(ss[:, 0:cols], ss[:, 0:cols]).then_inc(inverted[stage], 1)
                dve.wait_ge(inverted[stage], 1)

            def diagonals(stage, tiles):
                for n in range(tiles):
                    dve.tensor_scalar(diag[:, n, :], ident[:], ss[:, n:n + 1], None, ALU.mult)\
                       .then_inc(normed[stage], 1)

            def turn_lo(stage):
                for k in range(KD):
                    dve.wait_ge(t_hi[stage], k + 1)
                    dve.scalar_tensor_tensor(out=actT_lo[:, k, :], in0=ps[:, k % NBANK, :],
                                             scalar=gains[:, stage, k:k + 1], in1=actT_hi[:, k, :].bitcast(F32),
                                             op0=ALU.mult, op1=ALU.subtract).then_inc(t_lo[stage], 1)

            inverse_rms(IN_NORM, TT, D, TT)
            dve.wait_ge(s_const, 10)
            diagonals(IN_NORM, TT)
            dve.wait_ge(s_par, 16 * 7)
            turn_lo(IN_NORM)

            def sum_squares(c, part, cc):
                for t in range(TT):
                    dve.wait_ge(squared, 4 * c + (t + 1 + 8))
                    dve.tensor_reduce(stats[:, bass.ds(part, 1), t, 4 * cc:4 * cc + 4].rearrange("p a h -> p (a h)"),
                                      sq[:, t % 2, :].rearrange("p (h c) -> p h c", c=HD), AX_X, ALU.add)\
                       .then_inc(reduced, 1)

            make_lo(0, 0)
            with dve.Fori(0, PARTS) as i:
                for cc in range(2):
                    for kq in range(KQ):
                        n = 4 * cc + kq + 1
                        make_lo(8 * i + n, n % 2)
                    sum_squares(2 * i + cc, i, cc)
            st = stats[:].rearrange("p a t h -> p (a t h)")
            dve.wait_ge(reduced, 4 * IN_CHUNKS + 2)
            dve.tensor_scalar(st, st, 1.0 / HD, EPS, ALU.mult, ALU.add).then_inc(st_var, 1)
            dve.tensor_scalar(qgain, qgain, SCALE, None, ALU.mult).then_inc(st_inv, 1)
            dve.wait_ge(st_root, 1)
            dve.reciprocal(st, st).then_inc(st_inv, 1)
            dve.wait_ge(st_inv, 2)

            dve.wait_ge(s_sgp, 32)
            dve.memset(sgw_s[64:128, :, 0:64], 0.0).then_inc(s_sgm, 1)
            for h in range(HEADS):
                cols = slice(h * HD, (h + 1) * HD)
                for t in range(TT):
                    dve.scalar_tensor_tensor(out=proj[:, G_PART, t, cols], in0=proj[:, G_PART, t, cols],
                                             scalar=stats[:, G_PART, t, h:h + 1], in1=sgn_s[:, cols],
                                             op0=ALU.mult, op1=ALU.mult).then_inc(vb_made, 1)
            for h in range(HEADS):
                cols = slice(h * HD, (h + 1) * HD)
                dve.wait_ge(mixed, h + 1)
                dve.scalar_tensor_tensor(out=proj[:, U_PART, :, cols],
                                         in0=ps[:, h, :].rearrange("p (t c) -> p t c", t=TT),
                                         scalar=sgb_s[:, h:h + 1], in1=proj[:, U_PART, :, cols],
                                         op0=ALU.add, op1=ALU.mult).then_inc(gated, 1)

            def norm_qk(i):
                for ab in range(2):
                    n = 2 * i + ab
                    for j in range(2):
                        r = stats[:, j, :, bass.ds(n, 1)]
                        dve.tensor_tensor(qk_n[:, ab, j, :, :], proj[:, j, :, bass.ds(n * HD, HD)],
                                          r.broadcast_to([P, TT, HD]), ALU.mult).then_inc(qk_normed, 1)

            def attend(i, last):
                if not last:
                    dve.wait_ge(qk_turned, 4 * i + 4)
                    norm_qk(i + 1)
                for ab in range(2):
                    n = 2 * i + ab
                    z = ps[:, 1 + 3 * ab:4 + 3 * ab, :].rearrange("p b n -> p (b n)")
                    dve.wait_ge(z_ln, n + 1)
                    dve.scalar_tensor_tensor(out=sp[:, ab, :], in0=z[:, 0:1280], scalar=0.0, in1=sp_t[:, ab, :],
                                             op0=ALU.max, op1=ALU.add).then_inc(sp_made, 1)
                    dve.wait_ge(sp_made, n + 1)
                    three = sp[:, ab, 0:1280].rearrange("p (b n) -> p b n", n=256)[:, 0:5:2, 0:P]
                    dve.tensor_tensor(three, three, bcast(keep[:], [P, 3, P], 1), ALU.mult).then_inc(sp_kept, 1)
                    dve.tensor_tensor(sp[:, ab, 896:1024], sp[:, ab, 896:1024], keep[:], ALU.mult)\
                       .then_inc(sp_kept, 1)
                for ab in range(2):
                    n = 2 * i + ab
                    z = ps[:, 1 + 3 * ab:4 + 3 * ab, :]
                    dve.wait_ge(tails, n + 1)
                    dve.tensor_tensor(z[:, :, 0:P], z[:, :, 0:P], bcast(block_m[:], [P, 3, P], 1), ALU.add)\
                       .then_inc(z_blocked, 1)
                    dve.tensor_tensor(z[:, 1, 384:512], z[:, 1, 384:512], block_m[:], ALU.add)\
                       .then_inc(z_blocked, 1)

            with dve.Fori(0, 1) as i:
                norm_qk(i)
            with dve.Fori(0, HEADS // 2 - 1) as i:
                attend(i, False)
            with dve.Fori(HEADS // 2 - 1, HEADS // 2) as i:
                attend(i, True)

            inverse_rms(MIX_NORM, 2 * TT, WIDTH, 2 * TT)
            diagonals(MIX_NORM, 2 * TT)
            turn_lo(MIX_NORM)
            dve.wait_ge(s_x1, 16)
            with dve.Fori(0, 2) as i:
                for cc in range(2):
                    for kq in range(KQ):
                        n = 4 * cc + kq + 1
                        make_lo(8 * i + (P_OUT + n), n % 2)
                    dve.wait_ge(ring_free, 8 * i + (P_OUT + 4 * cc + 4 + RING_SLOTS))
                    for t in range(TT):
                        col = x1[:, t, bass.ds(i * 2 * BANK + cc * BANK, BANK)]
                        dve.tensor_tensor(col, ps[:, cc * 4 + t, :], col, ALU.add).then_inc(out_added, 1)
            dve.wait_ge(row_sq[FFN_NORM], TT * KQ)
            dve.tensor_reduce(ss[:, 0:TT], ss_part, AX_X, ALU.add).then_inc(row_sq[FFN_NORM], 1)
            inverse_rms(FFN_NORM, TT, D, TT * KQ + 1)
            diagonals(FFN_NORM, TT)
            turn_lo(FFN_NORM)

            for c in range(4):
                for kq in range(KQ):
                    m = 4 * c + kq + 1
                    if m < MM_PIECES:
                        make_lo(P_QUERY + m, m % 2)
                for h in range(2 * c, 2 * c + 2):
                    dve.wait_ge(q_sq, 2 * h + 2)
                    dve.tensor_tensor(sqh[:, h, :], sq[:, 0, :], sq[:, 1, :], ALU.add).then_inc(q_pair, 1)
            dve.wait_ge(q_ss, 1)
            dve.tensor_scalar(rq, ps[:, 7, 0:TT * PH].rearrange("p (t h) -> p t h", t=TT), -1.0 / (2 * HD), EPS,
                              ALU.mult, ALU.add).then_inc(q_var, 1)
            dve.wait_ge(q_root, 1)
            dve.reciprocal(rq, rq).then_inc(q_inv, 1)
            dve.wait_ge(q_inv, 1)

            STEPS = 22

            def retrieve(m, t, far):
                step = [0]

                def done(ins):
                    step[0] += 1
                    ins.then_inc(topk, 1)
                    dve.wait_ge(topk, STEPS * m + step[0])

                def carry():
                    dve.memset(tick, 0.0)

                def top16(count, values, best, places):
                    for half in range(2):
                        eight = slice(8 * half, 8 * half + 8)
                        for what in (0, 1, 2) if not half else (0, 1):
                            carry()
                            for n in range(count):
                                if what == 0:
                                    last = dve.max(best(n)[:, eight], values(n))
                                elif what == 1:
                                    last = dve.max_index(places(n)[:, eight], best(n)[:, eight], values(n))
                                else:
                                    last = dve.match_replace(values(n), best(n)[:, eight], values(n), NEG)
                            done(last)

                dve.wait_ge(s_done, m + 1)
                r = rq[:, bass.ds(t, 1), :].rearrange("p a h -> p (a h)")
                dve.tensor_tensor(s_sb[:].rearrange("p (h two) n -> p h (two n)", two=2),
                                  ps[:, 2:6, :].rearrange("p b (h n) -> p (b h) n", h=2),
                                  bcast(r, [P, PH, 2 * NK], 2), ALU.mult).then_inc(s_out, 1)
                dve.wait_ge(s_out, m + 1)
                top16(2 * PH, lambda n: s_sb[:, n, :], lambda n: v12[:, n, :], lambda n: i12u[:, n, :])
                v = v12[:].rearrange("p (h two) k -> p h two k", two=2)
                shape = [P, PH, TOPK, TOPK]
                done(dve.tensor_tensor(cand[:], bcast(v[:, :, 0, :], shape, 3), bcast(v[:, :, 1, :], shape, 2),
                                       ALU.add))
                flat = cand[:].rearrange("p h a b -> p h (a b)")
                top16(PH, lambda n: flat[:, n, :], lambda n: tv[:, n, :], lambda n: tpos[:, n, :])
                done(dve.tensor_tensor(gate_e[:], tv[:], tv[:, :, 0:1].broadcast_to([P, PH, TOPK]), ALU.subtract))
                dve.tensor_copy(i12f[:], i12u[:]).then_inc(sm_sub, 1)
                pos = tpos[:].rearrange("p h k -> p (h k)")
                dve.tensor_scalar(posu[:, 0, :], pos, 4, None, ALU.logical_shift_right)
                done(dve.tensor_scalar(posu[:, 1, :], pos, 15, None, ALU.bitwise_and))
                done(dve.tensor_copy(posf[:], posu[:]))
                full = [P, PH * TOPK, TOPK]
                idx = i12f[:].rearrange("p (h two) a -> p h two a", two=2)
                eq4 = eq[:].rearrange("p (h k) a -> p h k a", h=PH)
                for j in range(2):
                    done(dve.tensor_tensor(eq[:], bcast(iota16[:], full, 1), bcast(posf[:, j, :], full, 2),
                                           ALU.is_equal))
                    done(dve.tensor_tensor(eq4, eq4, bcast(idx[:, :, j, :], [P, PH, TOPK, TOPK], 2), ALU.mult))
                    done(dve.tensor_reduce(sel[:, j, :], eq[:], AX_X, ALU.add))
                dve.wait_ge(sm_exp, m + 1)
                done(dve.tensor_reduce(gate_s[:, 0, :], gate_e[:], AX_X, ALU.add))
                done(dve.reciprocal(gate_s[:, 1, :], gate_s[:, 0, :]))
                dst = gate_far[:] if far else sel[:, 2, :]
                dve.tensor_tensor(dst.rearrange("p (h k) -> p h k", h=PH), gate_e[:],
                                  bcast(gate_s[:, 1, :], [P, PH, TOPK], 2), ALU.mult)\
                   .then_inc(far_sel if far else sel_made, 1)
                if far:
                    dve.scalar_tensor_tensor(out=idx_far[:], in0=sel[:, 0, :], scalar=float(NK), in1=sel[:, 1, :],
                                             op0=ALU.mult, op1=ALU.add).then_inc(far_sel, 1)
                    dve.wait_ge(far_sel, 2)
                else:
                    dve.wait_ge(sel_turned, t + 1)
                    dve.tensor_copy(selT[:, :, bass.ds(t * P, P)],
                                    ps[:, 6, 0:3 * P].rearrange("p (s n) -> p s n", s=3)).then_inc(selT_out, 1)
                assert step[0] == STEPS

            with dve.Fori(0, 1) as m:
                retrieve(m, m + FAR, True)
            with dve.Fori(0, NT) as t:
                retrieve(t + 1, t, False)
            dve.wait_ge(selT_out, NT)

            def hot(b, j):
                dve.wait_ge(g_mm, 16 * b + (j + 1))
                for q in range(4):
                    m = 4 * (j % 4) + q
                    tok = bass.ds(GSTEP * b + (4 * j + q), 1)
                    dve.tensor_scalar(hot_a[:, m, :], iota[:], selT[:, 0, tok], selT[:, 2, tok],
                                      ALU.is_equal, ALU.mult)
                    last = dve.tensor_scalar(hot_b[:, m, :], iota[:], selT[:, 1, tok], None, ALU.is_equal)
                last.then_inc(hot_made, 1)

            with dve.Fori(0, NEAR // GSTEP) as b:
                for j in range(16):
                    hot(b, j)

            blocks = "p (k c) -> p k c"

            def gate(i, par, c, src, use):
                dve.wait_ge(g_loaded[c // 2], 16 * use)
                by_step = src.rearrange("p b (s t) -> p b s t", t=GSTEP)
                dve.tensor_tensor(by_step, by_step, g_pair[c // 2].rearrange(
                    "p (b s) (i t) -> p b s i t", s=P // GSTEP, i=2)[:, :, :, c % 2, :], ALU.mult).then_inc(act_made, 1)
                dve.wait_ge(ahi_made, i + 1)
                dst = a_lo[par][:, c, :].rearrange("p (b t) -> p b t", t=P)
                dve.tensor_tensor(dst, src, a_hi[:, par, c, :].bitcast(F32).rearrange("p (b t) -> p b t", t=P),
                                  ALU.subtract).then_inc(alo_made, 1)

            def add_out(p, c):
                dve.wait_ge(ring_free, p + (1 + RING_SLOTS))
                for t in range(NT):
                    col = x1[:, t, c * BANK:(c + 1) * BANK]
                    dve.tensor_tensor(col, ps[:, 2 + 3 * (c % 2) + t, :], col, ALU.add).then_inc(y_added, 1)

            def use_rows(parts, part, q, b):
                n = sum(len(x) for x in parts[:part])
                for kind, batch, slot in parts[part]:
                    buf, col = n % GATHER_BUFS, BATCH * batch + slot
                    row = rows[buf][:]
                    if kind == "v" and slot == 0:
                        cols = a_far[:, BATCH * batch:BATCH * (batch + 1)]
                        dve.wait_ge(far_gelu, b + (batch + 1))
                        dve.tensor_tensor(cols, cols, gate_far[:, bass.ds(BATCH * b + BATCH * batch, BATCH)], ALU.mult)\
                           .then_inc(far_weight, 1)
                        dve.wait_ge(far_weight, b + (batch + 1))
                    gath = (q + (n - buf)) * (16 // GATHER_BUFS) + 16
                    if kind == "u":
                        dve.wait_ge(gathered[buf], gath)
                        row = row.rearrange(blocks, c=P)
                        dve.tensor_tensor_reduce(out=row, in0=row, in1=h_far, scale=1.0, scalar=0.0, op0=ALU.mult,
                                                 op1=ALU.add, accum_out=z_far[:, col:col + 1]).then_inc(row_used, 1)
                    else:
                        dve.wait_ge(row_used, q + (n + GATHER_BUFS))
                        dve.wait_ge(gathered[buf], gath)
                        dve.scalar_tensor_tensor(out=x1[:, FAR, :], in0=row, scalar=a_far[:, col:col + 1],
                                                 in1=x1[:, FAR, :], op0=ALU.mult, op1=ALU.add).then_inc(row_used, 1)
                    n += 1

            def down_group(g, par, part, parts, q, b):
                for c in range(GROUP):
                    p = 4 * g + (c + P_DOWN - GROUP)
                    make_lo(p + 1, (c + 1) % 2)
                    dve.wait_ge(gin_loaded[c % 2], 32 * g + (16 * (c // 2) + 16))
                    gate(4 * g + c, par, c, g_in[c % 2], g + 1)
                    use_rows(parts, part + c, q, b)
                    add_out(p, c)

            def both_group(g, par, part, q, b):
                for c in range(GROUP):
                    p = 8 * g + (2 * c + P_BOTH - 8 * PRE_GROUPS)
                    make_lo(p + 1, 1)
                    use_rows(BOTH_GATHERS, part + c, q, b)
                    make_lo(p + 2, 0)
                    dve.wait_ge(gelu_made, 4 * g + (c + 3))
                    gate(4 * g + c, par, c, gelu[:, c % 2, :].rearrange("p (b t) -> p b t", t=P), g + 1)
                    add_out(p + 1, c)

            for c in range(GROUP):
                dve.wait_ge(gin_loaded[c % 2], 16 * (c // 2) + 16)
                gate(c, 0, c, g_in[c % 2], 1)
            for b in range(2):
                dve.wait_ge(ahead_stored[b], 16 * (PRE // 2) + 16)
            dve.wait_ge(nf_loaded, 16)
            dve.scalar_tensor_tensor(out=h_far, in0=x1[:, FAR, :].rearrange(blocks, c=P), scalar=ss[:, FAR:FAR + 1],
                                     in1=rows[0][:].rearrange(blocks, c=P), op0=ALU.mult, op1=ALU.mult)\
               .then_inc(h_far_made, 1)
            dve.wait_ge(h_far_made, 1)
            dve.wait_ge(lo_made, P_DOWN + 1)
            with dve.Fori(0, PRE_GROUPS // 2 - 1) as r:
                down_group(2 * r + 1, 1, 0, DOWN_GATHERS, 8 * r, r)
                down_group(2 * r + 2, 0, 4, DOWN_GATHERS, 8 * r, r)
            with dve.Fori(PRE_GROUPS - 1, PRE_GROUPS) as g:
                down_group(g, 1, 0, TAIL_GATHERS, 8 * g - 8 * (PRE_GROUPS - 1) + 4 * PRE_GROUPS - 8,
                           g - (PRE_GROUPS - 1) + (PRE_GROUPS // 2 - 1))
            with dve.Fori(0, (N_GROUPS - PRE_GROUPS) // 2) as r:
                q, b = 24 * r + 4 * PRE_GROUPS, 3 * r + PRE_GROUPS // 2
                both_group(2 * r + PRE_GROUPS, 0, 0, q, b)
                both_group(2 * r + (PRE_GROUPS + 1), 1, 4, q, b)
            for c in range(GROUP):
                if c:
                    make_lo(P_LAST + c, c % 2)
                add_out(P_LAST + c, c)

        @block.tensor
        def _(pe):
            def three(dst, w_h, w_l, m_h, m_l, first, last):
                pe.matmul(dst, w_h, m_h, start=first, stop=False)
                pe.matmul(dst, w_h, m_l, start=False, stop=False)
                return pe.matmul(dst, w_l, m_h, start=False, stop=last)

            def turn(stage, sources):
                pe.wait_ge(normed[stage], sources)
                for k in range(KD):
                    if k >= NBANK:
                        pe.wait_ge(t_lo[stage], k - NBANK + 1)
                    for t in range(TT):
                        block, rows_diag = turned_from(stage, t, k)
                        last = pe.matmul(ps[:, k % NBANK, t * P:(t + 1) * P], block, rows_diag, start=True, stop=True)
                    last.then_inc(turned[stage], 1)
                pe.wait_ge(t_lo[stage], KD)

            def rows_piece(p, slot, kq, bank):
                pe.wait_ge(lo_made, p + 1)
                for kk in range(4):
                    k = 4 * kq + kk
                    cols = slice(kk * BANK, (kk + 1) * BANK)
                    for t in range(TT):
                        a = slice(t * P, (t + 1) * P)
                        last = three(ps[:, bank + t, :], actT_hi[:, k, a], actT_lo[:, k, a],
                                     hi[:, slot, cols], lo[:, slot, cols], k == 0, k == KD - 1)
                last.then_inc(ring_free, 1)
                return last

            pe.sem_inc(ring_free, RING_SLOTS)
            pe.sem_inc(squared, 8)
            pe.wait_ge(s_const, 10)
            turn(IN_NORM, TT)
            with pe.Fori(0, PARTS) as i:
                for cc in range(2):
                    pe.wait_ge(squared, 8 * i + (4 * cc + 4))
                    for kq in range(KQ):
                        rows_piece(8 * i + (4 * cc + kq), kq % 2, kq, 4 * cc)

            pe.wait_ge(s_sgm, 1)
            pe.wait_ge(squared, 8 + 4 * IN_CHUNKS)
            for h in range(HEADS):
                pe.wait_ge(vb_made, TT * (h + 1))
                pe.matmul(ps[:, h, :], sgw_s[:, h, :], proj[:, G_PART, :, h * HD:(h + 1) * HD],
                          start=True, stop=True).then_inc(mixed, 1)

            Z_AT = ((0, 0), (1, 0), (2, 0), (1, 384))
            pe.wait_ge(gated, HEADS)
            pe.sem_inc(y_out, 1)

            def turn_qk(i):
                for ab in range(2):
                    n = 2 * i + ab
                    for j in range(2):
                        pe.wait_ge(qk_normed, 2 * n + (j + 1))
                        if ab:
                            pe.wait_ge(qkT_out, 4 * i + (j + 1))
                        for t in range(TT):
                            last = pe.transpose(ps[:, 7 * j, t * P:(t + 1) * P], qk_n[:, ab, j, t, :], ident[:])
                        last.then_inc(qk_turned, 1)

            def attend(i, is_last):
                for ab in range(2):
                    n = 2 * i + ab
                    pe.wait_ge(qkT_out, 2 * n + 2)
                    for b in range(TT):
                        bank, col = Z_AT[b]
                        last = pe.matmul(ps[:, 1 + 3 * ab + bank, col:col + SEQ - b * P],
                                         qkT[:, ab, 1, b * P:(b + 1) * P], qkT[:, ab, 0, b * P:SEQ],
                                         start=(b < 3), stop=True, skip_group_check=True)
                    last.then_inc(z_done, 1)
                if not is_last:
                    pe.wait_ge(y_out, 2 * i + 1)
                    turn_qk(i + 1)
                for ab in range(2):
                    n = 2 * i + ab
                    pe.wait_ge(sp_kept, 2 * n + 2)
                    for b in range(TT):
                        bank, col = Z_AT[b]
                        for b2 in range(b, TT):
                            bank2, col2 = Z_AT[b2]
                            width = SEQ - b2 * P
                            at2 = bank2 * BANK + col2
                            off = col + (b2 - b) * P
                            last = pe.matmul(ps[:, 1 + 3 * ab + bank, off:off + width],
                                             tri[:] if b2 == b else neg1[:], sp[:, ab, at2:at2 + width],
                                             start=False, stop=True, skip_group_check=True)
                    last.then_inc(tails, 1)
                for ab in range(2):
                    n = 2 * i + ab
                    pe.wait_ge(w_made, n + 1)
                    pe.wait_ge(v_copied, n + 1)
                    if not ab:
                        pe.wait_ge(qkT_out, 4 * i + (4 if is_last else 8))
                    for t in range(TT):
                        for b in range(t + 1):
                            bank, col = Z_AT[b]
                            at1 = bank * BANK + col + (t - b) * P
                            last = pe.matmul(ps[:, 7 * ab, t * P:(t + 1) * P], w_att[:, ab, at1:at1 + P],
                                             v_h[:, ab, b, :], start=(t == 0 and b == 0), stop=(b == t),
                                             skip_group_check=True)
                    last.then_inc(pv_done, 1)

            with pe.Fori(0, 1) as i:
                turn_qk(i)
            with pe.Fori(0, HEADS // 2 - 1) as i:
                attend(i, False)
            with pe.Fori(HEADS // 2 - 1, HEADS // 2) as i:
                attend(i, True)

            turn(MIX_NORM, 2 * TT)
            pe.sem_inc(out_added, 8)
            with pe.Fori(0, 2) as i:
                for cc in range(2):
                    pe.wait_ge(out_added, 8 * i + (4 * cc + 4))
                    for kq in range(KQ):
                        rows_piece(8 * i + (P_OUT + 4 * cc + kq), kq % 2, kq, 4 * cc)
            turn(FFN_NORM, TT)

            for c in range(4):
                if c >= 2:
                    pe.wait_ge(q_out, 4 * (c - 1))
                    pe.wait_ge(q_sq, 4 * (c - 1))
                for kq in range(KQ):
                    m = 4 * c + kq
                    pe.wait_ge(lo_made, P_QUERY + m + 1)
                    for kk in range(4):
                        k = 4 * kq + kk
                        for b in range(4):
                            col = slice(kk * BANK + b * P, kk * BANK + (b + 1) * P)
                            last = three(ps[:, 4 * (c % 2) + b, :], hi[:, m % 2, col], lo[:, m % 2, col],
                                         actT_hi[:, k, :], actT_lo[:, k, :], k == 0, k == KD - 1)
                    last.then_inc(ring_free, 1)
            def up(p, slot, i, z_bank):
                pe.wait_ge(gelu_made, i + 1)
                pe.wait_ge(lo_made, p + 1)
                for k in range(KD):
                    e = slice(k * P, (k + 1) * P)
                    last = three(ps[:, z_bank, 0:NEAR], hi[:, slot, e], lo[:, slot, e], actT_hi[:, k, 0:NEAR],
                                 actT_lo[:, k, 0:NEAR], k == 0, k == KD - 1)
                last.then_inc(ring_free, 1)

            def scores(m, t):
                if m:
                    pe.wait_ge(s_out, m)
                for n in range(2 * PH):
                    last = pe.matmul(ps[:, 2 + n // 4, (n % 4) * NK:(n % 4 + 1) * NK], qT[:, n, t * P:(t + 1) * P],
                                     keysT[:, n % 2, :], start=True, stop=True)
                last.then_inc(s_done, 1)

            pe.sem_inc(gelu_made, 2)
            pe.sem_inc(g_mm, 4)
            pe.sem_inc(g_out, 4)
            pe.sem_inc(y_added, 6)
            pe.sem_inc(row_used, GATHER_BUFS)

            def up_pairs(first, end):
                with pe.Fori(first, end) as h:
                    for b in range(2):
                        up(2 * h + (P_PEER + b), b, 2 * h + b, b)

            up_pairs(0, 1)
            pe.wait_ge(q_pair, PH)
            pe.wait_ge(q_out, 16)
            for t in range(TT):
                for h in range(PH):
                    col = t * PH + h
                    last = pe.matmul(ps[:, 7, col:col + 1], sqh[:, h, t * P:(t + 1) * P], neg1[:, 0:1],
                                     start=True, stop=True)
            last.then_inc(q_ss, 1)
            scores(0, FAR)
            up_pairs(1, AHEAD_FAR // 2)
            scores(1, 0)
            first = AHEAD_FAR // 2
            for t in range(NT):
                end = first + AHEAD_NEAR[t] // 2
                up_pairs(first, end - 1)
                if t + 1 < NT:
                    scores(t + 2, t + 1)
                up_pairs(end - 1, end)
                first = end
                pe.wait_ge(sel_made, t + 1)
                if t:
                    pe.wait_ge(selT_out, t)
                for j in range(3):
                    last = pe.transpose(ps[:, 6, j * P:(j + 1) * P], sel[:, j, :], ident[:])
                last.then_inc(sel_turned, 1)

            def outers(b, quad):
                for j in range(4 * quad, 4 * quad + 4):
                    pe.wait_ge(hot_made, 16 * b + (j + 1))
                    pe.wait_ge(g_out, 16 * b + (j + 1))
                    for q in range(4):
                        m = 4 * (j % 4) + q
                        last = pe.matmul(ps[:, 2 + j % 4, q * NK:(q + 1) * NK], hot_b[:, m, :], hot_a[:, m, :],
                                         start=True, stop=True)
                    last.then_inc(g_mm, 1)

            with pe.Fori(0, NEAR // GSTEP // 2) as r:
                for s in range(2):
                    b = 2 * r + s

                    def up_of(n):
                        at = AHEAD_1 + AHEAD_GATES * s + n
                        up(2 * AHEAD_GATES * r + (at + P_PEER), at % 2, 2 * AHEAD_GATES * r + at, at % 2)

                    up_of(0)
                    outers(b, 0)
                    up_of(1)
                    for quad in range(1, 4):
                        up_of(quad + 1)
                        outers(b, quad)
            up_pairs(AHEAD_2 // 2, PRE // 2)
            pe.wait_ge(g_out, 4 + NEAR // 4)

            def down(p, slot, g, c, par):
                pe.wait_ge(lo_made, p + 1)
                if c == 0:
                    pe.wait_ge(alo_made, 4 * g + 4)
                pe.wait_ge(y_added, 12 * g + (3 * c + 3))
                for e in range(GROUP):
                    cols = slice(e * BANK, (e + 1) * BANK)
                    for t in range(NT):
                        a = slice(t * P, (t + 1) * P)
                        last = three(ps[:, 2 + 3 * (c % 2) + t, :], a_hi[:, par, e, a], a_lo[par][:, e, a],
                                     hi[:, slot, cols], lo[:, slot, cols], e == 0, e == GROUP - 1)
                last.then_inc(ring_free, 1)

            def down_group(g, par):
                for c in range(GROUP):
                    down(4 * g + (c + P_DOWN - GROUP), c % 2, g - 1, c, 1 - par)

            def both_group(g, par):
                for c in range(GROUP):
                    p = 8 * g + (2 * c + P_BOTH - 8 * PRE_GROUPS)
                    up(p, 0, 4 * g + c, c % 2)
                    down(p + 1, 1, g - 1, c, 1 - par)

            with pe.Fori(0, PRE_GROUPS // 2 - 1) as r:
                down_group(2 * r + 1, 1)
                down_group(2 * r + 2, 0)
            down_group(PRE_GROUPS - 1, 1)
            with pe.Fori(0, (N_GROUPS - PRE_GROUPS) // 2) as r:
                both_group(2 * r + PRE_GROUPS, 0)
                both_group(2 * r + (PRE_GROUPS + 1), 1)
            for c in range(GROUP):
                down(P_LAST + c, c % 2, N_GROUPS - 1, c, 1)


def kernel(x, norm_mix, w_in, q_norm, k_norm, sg_norm, sg_w, sg_b, out_norm_sb, out_norm_sg,
           w_out, norm_ffn, peer_w_query, peer_sub_keys, peer_u, peer_v):
    import numpy as np
    import concourse.bacc as bacc
    from concourse.bass_utils import run_bass_kernel_spmd

    def laid(a, *axes):
        return np.ascontiguousarray(np.transpose(a, axes) if axes else a)

    def pieces(w):
        n = w.shape[1] // BANK
        return laid(np.reshape(w, (KQ, 4, P, n, BANK)), 3, 0, 2, 1, 4).reshape(n * KQ, P, PIECE)

    def by_block(g):
        return laid(np.reshape(g, (-1, P)), 1, 0)

    f = np.asarray
    arrays = {
        "x": laid(f(x)[0]),
        "norm_mix": by_block(f(norm_mix)[0]),
        "norm_ffn": by_block(f(norm_ffn)[0]),
        "norm_y": by_block(np.concatenate([f(out_norm_sb)[0], f(out_norm_sg)[0]])),
        "q_norm": laid(f(q_norm)[0].reshape(P, 1)),
        "k_norm": laid(f(k_norm)[0].reshape(P, 1)),
        "sg_norm": laid(np.broadcast_to(f(sg_norm)[0].reshape(1, WIDTH), (P, WIDTH))),
        "sg_w": laid(f(sg_w)[0], 2, 0, 1),
        "sg_b": laid(f(sg_b)[0], 1, 0),
        "keys": laid(f(peer_sub_keys)[0], 2, 0, 1),
        "w_in": pieces(f(w_in)[0]),
        "w_out": pieces(f(w_out)[0]),
        "w_query": pieces(f(peer_w_query)[0]),
        "peer_u": laid(np.reshape(f(peer_u)[0], (NK, P, KD, P)), 0, 3, 2, 1).reshape(NK, P, PIECE),
        "peer_u_rows": laid(f(peer_u)[0]),
        "peer_v": laid(f(peer_v)[0]),
        "norm_ffn_rows": laid(np.broadcast_to(f(norm_ffn)[0].reshape(1, D), (P, D))),
    }
    nc = bacc.Bacc("TRN2", target_bir_lowering=False, num_devices=1)
    args = [nc.dram_tensor(n, a.shape, mybir.dt.from_np(a.dtype), kind="ExternalInput").ap()
            for n, a in arrays.items()]
    out = nc.dram_tensor("y", (SEQ, D), F32, kind="ExternalOutput").ap()
    layer(nc, *args, out)
    r = run_bass_kernel_spmd(nc, [arrays], core_ids=[0])
    return r.results[0]["y"].reshape(1, SEQ, D)
```
